# Optimizing a Trainium2 kernel written in Bass

```python
import math
import jax, jax.numpy as jnp
from jax import lax
import numpy as np

D_MODEL = 2048
BATCH = 1
SEQ = 512
DEPTH = 1

CHUNK = 64
Q_BLOCK = 128
HEAD_DIM = 128
N_FOX_HEADS = 8
N_SB_HEADS = 8
D_FOX = N_FOX_HEADS * HEAD_DIM
D_SB = N_SB_HEADS * HEAD_DIM
D_MIX = D_FOX + D_SB
D_IN = 4 * D_FOX + 3 * D_SB + N_FOX_HEADS
N_KEYS = 128
N_EXPERTS = N_KEYS * N_KEYS
PEER_HEADS = 8
PEER_TOPK = 16
PEER_DKEY = 256
PEER_HALF = PEER_DKEY // 2
PEER_TOK_BLOCK = 128
EPS = 1e-6

kernel_name = "fox_stickbreak_peer_hybrid_block"

def rmsnorm(x, g):
    xf = x.astype(jnp.float32)
    r = lax.rsqrt(jnp.mean(xf * xf, axis=-1, keepdims=True) + EPS)
    return (xf * r).astype(x.dtype) * g

def fox_block(q_blk, k_ctx, v_ctx, c_q, c_k, t0):
    logits = jnp.einsum('bhqd,bhkd->bhqk', q_blk, k_ctx,
                        preferred_element_type=jnp.float32) * (HEAD_DIM ** -0.5)
    logits = logits + c_q[..., :, None] - c_k[..., None, :]
    tq = t0 + jnp.arange(q_blk.shape[2])
    tk = jnp.arange(k_ctx.shape[2])
    mask = tk[None, :] <= tq[:, None]
    logits = jnp.where(mask, logits, -jnp.inf)
    p = jax.nn.softmax(logits, axis=-1)
    return jnp.einsum('bhqk,bhkd->bhqd', p.astype(v_ctx.dtype), v_ctx)

def stick_breaking_block(q_blk, k_ctx, v_ctx, t0):
    z = jnp.einsum('bhqd,bhkd->bhqk', q_blk, k_ctx,
                   preferred_element_type=jnp.float32) * (HEAD_DIM ** -0.5)
    tq = t0 + jnp.arange(q_blk.shape[2])
    tk = jnp.arange(k_ctx.shape[2])
    mask = tk[None, :] < tq[:, None]
    log_beta = jax.nn.log_sigmoid(z)
    log_1mb = jnp.where(mask, jax.nn.log_sigmoid(-z), 0.0)
    suffix = lax.cumsum(log_1mb, axis=3, reverse=True) - log_1mb
    a = jnp.where(mask, jnp.exp(log_beta + suffix), 0.0)
    return jnp.einsum('bhqk,bhkd->bhqd', a.astype(v_ctx.dtype), v_ctx)

def hybrid_mixer(xn, w_in, b_forget, q_norm_g, k_norm_g, w_out):
    B, S, _ = xn.shape
    proj = xn @ w_in

    def heads(t, n_heads):
        return t.reshape(B, S, n_heads, HEAD_DIM).transpose(0, 2, 1, 3)

    o = 0
    q_f = rmsnorm(heads(proj[..., o:o + D_FOX], N_FOX_HEADS), q_norm_g); o += D_FOX
    k_f = rmsnorm(heads(proj[..., o:o + D_FOX], N_FOX_HEADS), k_norm_g); o += D_FOX
    v_f = heads(proj[..., o:o + D_FOX], N_FOX_HEADS); o += D_FOX
    gate_f = jax.nn.sigmoid(proj[..., o:o + D_FOX]); o += D_FOX
    q_s = heads(proj[..., o:o + D_SB], N_SB_HEADS); o += D_SB
    k_s = heads(proj[..., o:o + D_SB], N_SB_HEADS); o += D_SB
    v_s = heads(proj[..., o:o + D_SB], N_SB_HEADS); o += D_SB
    f_logit = proj[..., o:o + N_FOX_HEADS].astype(jnp.float32) + b_forget
    log_f = jax.nn.log_sigmoid(f_logit)
    c = jnp.cumsum(log_f, axis=1).transpose(0, 2, 1)

    fox_out, sb_out = [], []
    for i in range(S // Q_BLOCK):
        t0 = i * Q_BLOCK
        end = t0 + Q_BLOCK
        fox_out.append(fox_block(q_f[:, :, t0:end], k_f[:, :, :end], v_f[:, :, :end],
                                 c[:, :, t0:end], c[:, :, :end], t0))
        sb_out.append(stick_breaking_block(q_s[:, :, t0:end], k_s[:, :, :end],
                                           v_s[:, :, :end], t0))
    fox = jnp.concatenate(fox_out, axis=2).transpose(0, 2, 1, 3).reshape(B, S, D_FOX)
    sb = jnp.concatenate(sb_out, axis=2).transpose(0, 2, 1, 3).reshape(B, S, D_SB)
    mixed = jnp.concatenate([fox * gate_f, sb], axis=-1)
    return mixed @ w_out

def peer_ffn(xn, w_pq, sub_keys, u, v):
    B, S, D = xn.shape
    T = B * S
    xt = xn.reshape(T, D)
    q = (xt @ w_pq).reshape(T, PEER_HEADS, 2, PEER_HALF)
    s = jnp.einsum('thcd,hcnd->thcn', q, sub_keys,
                   preferred_element_type=jnp.float32)
    s1, i1 = lax.top_k(s[:, :, 0], PEER_TOPK)
    s2, i2 = lax.top_k(s[:, :, 1], PEER_TOPK)
    cand = (s1[..., :, None] + s2[..., None, :]).reshape(T, PEER_HEADS, PEER_TOPK * PEER_TOPK)
    cidx = (i1[..., :, None] * N_KEYS + i2[..., None, :]).reshape(T, PEER_HEADS, PEER_TOPK * PEER_TOPK)
    top_s, pos = lax.top_k(cand, PEER_TOPK)
    idx = jnp.take_along_axis(cidx, pos, axis=-1)
    g = jax.nn.softmax(top_s, axis=-1).astype(xn.dtype)
    n_blk = T // PEER_TOK_BLOCK
    E = PEER_HEADS * PEER_TOPK

    def block(args):
        xb, ib, gb = args
        ub = u[ib]
        h = jax.nn.gelu(jnp.einsum('ted,td->te', ub, xb), approximate=False)
        vb = v[ib]
        return jnp.einsum('te,ted->td', gb * h, vb)

    out = lax.map(block, (xt.reshape(n_blk, PEER_TOK_BLOCK, D),
                          idx.reshape(n_blk, PEER_TOK_BLOCK, E),
                          g.reshape(n_blk, PEER_TOK_BLOCK, E)))
    return out.reshape(B, S, D)

def setup_inputs(seed: int = 0) -> dict:
    key = jax.random.key(seed)
    ks = jax.random.split(key, 14)
    f32 = jnp.float32
    nrm = lambda k, shape, scale: jax.random.normal(k, shape, f32) * scale
    return {
        "x": jax.random.normal(ks[0], (BATCH, SEQ, D_MODEL), f32),
        "attn_norm_g": 1.0 + nrm(ks[1], (DEPTH, D_MODEL), 0.02),
        "w_in": nrm(ks[2], (DEPTH, D_MODEL, D_IN), D_MODEL ** -0.5),
        "b_forget": 3.0 + nrm(ks[3], (DEPTH, N_FOX_HEADS), 0.5),
        "q_norm_g": 1.0 + nrm(ks[4], (DEPTH, HEAD_DIM), 0.02),
        "k_norm_g": 1.0 + nrm(ks[5], (DEPTH, HEAD_DIM), 0.02),
        "w_out": nrm(ks[6], (DEPTH, D_MIX, D_MODEL), D_MIX ** -0.5),
        "ffn_norm_g": 1.0 + nrm(ks[7], (DEPTH, D_MODEL), 0.02),
        "w_peer_q": nrm(ks[8], (DEPTH, D_MODEL, PEER_HEADS * PEER_DKEY), D_MODEL ** -0.5),
        "peer_sub_keys": nrm(ks[9], (DEPTH, PEER_HEADS, 2, N_KEYS, PEER_HALF), PEER_HALF ** -0.5),
        "peer_u": nrm(ks[10], (DEPTH, N_EXPERTS, D_MODEL), D_MODEL ** -0.5),
        "peer_v": nrm(ks[11], (DEPTH, N_EXPERTS, D_MODEL), PEER_HEADS ** -0.5),
    }

def reference(x, attn_norm_g, w_in, b_forget, q_norm_g, k_norm_g, w_out,
              ffn_norm_g, w_peer_q, peer_sub_keys, peer_u, peer_v):
    h = x
    for l in range(DEPTH):
        xn = rmsnorm(h, attn_norm_g[l])
        h = h + hybrid_mixer(xn, w_in[l], b_forget[l], q_norm_g[l], k_norm_g[l], w_out[l])
        hn = rmsnorm(h, ffn_norm_g[l])
        h = h + peer_ffn(hn, w_peer_q[l], peer_sub_keys[l], peer_u[l], peer_v[l])
    return h


_drawn_inputs = setup_inputs


def setup_inputs(seed=0):
    import zlib

    import numpy as np

    out = dict(_drawn_inputs(seed))
    spreads = {}
    factors = {'q_norm_g': 7.606, 'k_norm_g': 6.608}
    for name, (base, spread) in spreads.items():
        noise = np.random.default_rng([zlib.crc32(name.encode()), seed]).standard_normal(out[name].shape)
        drawn = base * np.exp(spread * noise) if base else spread * noise
        out[name] = __import__('jax').numpy.asarray(drawn.astype(out[name].dtype))
    for name, factor in factors.items():
        out[name] = (out[name] * factor).astype(out[name].dtype)
    return out
```

```python
from contextlib import ExitStack

import concourse.bass as bass
from concourse import mybir

F32 = mybir.dt.float32
F32R = mybir.dt.float32r
BF16 = mybir.dt.bfloat16
U32 = mybir.dt.uint32
ALU = mybir.AluOpType
ACT = mybir.ActivationFunctionType
AX = mybir.AxisListType

P = 128
T = 512
D = 2048
TB = T // P
KC = D // P
HD = 128
NFOX = 8
NSB = 8
HEADS = NFOX + NSB
PH = 8
TOPK = 16
NKEYS = 128
GRP = 4
NGRP = NKEYS // GRP
CH = D // 512
LAG = 8
GT = 32
NGC = T // GT
EPS = 1e-6
SCALE = float(HD) ** -0.5
LOWEST = -3.0e38
MASKED = -1.0e30

N_FOX = 1
N_SB = N_FOX + 4 * NFOX
N_OUT = N_SB + 3 * NSB
N_PQ = N_OUT + CH * (HEADS // 4)
N_PRO = N_PQ + 2 * PH
N_MAIN = N_PRO + GRP * LAG
N_TAIL = N_MAIN + 2 * GRP * (NGRP - LAG)
N_END = N_TAIL + GRP * LAG
M_PQ = N_OUT
M_PRO = M_PQ + 2 * PH
M_MAIN = M_PRO + GRP * LAG

TOPK_STEPS = 23

FOX_OFF = [P * i * (i + 1) // 2 for i in range(TB + 1)]
COL_OFF = [0]
for _j in range(TB):
    COL_OFF.append(COL_OFF[-1] + P * (TB - _j))
TRI = FOX_OFF[TB]


def build(nc, x, attn_g, w_in, b_forget, q_g, k_g, w_out, ffn_g, w_pq, sub_keys, u, v, out):
    ctx = ExitStack()
    with ctx:
        def sb(name, shape, dt=F32):
            return ctx.enter_context(nc.sbuf_tensor(name, shape, dt))

        def sem(name):
            return ctx.enter_context(nc.semaphore(name))

        score_dram = nc.dram_tensor("score_scratch", [TB, P, 2 * PH * NKEYS], F32, kind="Internal").ap()
        gate_dram = nc.dram_tensor("gate_scratch", [NGC, P, NKEYS * GT], F32, kind="Internal").ap()
        act_dram = nc.dram_tensor("act_scratch", [NKEYS, P, T], F32, kind="Internal").ap()

        acc = sb("acc", [P, TB, D])
        mixed = acc[:].rearrange("p a b -> p (a b)")
        xh = sb("xh", [P, KC, T], F32R)
        xl = sb("xl", [P, KC, T], F32R)
        raw = [sb(f"raw{s}", [P, D]) for s in range(2)]
        wh = [sb(f"wh{s}", [P, D], F32R) for s in range(2)]
        wl = [sb(f"wl{s}", [P, D], F32R) for s in range(2)]
        gh = sb("gh", [P, GRP * T], F32R)
        gl = sb("gl", [P, GRP * T], F32R)
        gate_hi = sb("gate_hi", [P, P], F32R)

        ident = sb("ident", [P, P])
        ones = sb("ones", [P, P])
        neg_ones = sb("neg_ones", [P, P])
        neg_tri = sb("neg_tri", [P, P])
        strict = sb("strict", [P, P])
        iota128 = sb("iota128", [P, P])
        iota16 = sb("iota16", [P, TOPK])
        ident_b = sb("ident_b", [P, P], BF16)
        fox_mask = sb("fox_mask", [P, P], BF16)
        sb_mask = sb("sb_mask", [P, P], BF16)
        gains = sb("gains", [P, 2, KC])
        qk_gain = sb("qk_gain", [P, 3])
        bf = sb("bf", [PH, 1])
        eps = sb("eps", [P, 1])
        stat = sb("stat", [P, 16])
        fox_stat = sb("fox_stat", [P, 16])
        carry = sb("carry", [P, 96])
        carried = [0]

        arena = sb("arena", [P, 10700])

        def at(o, n, parts=P):
            return arena[0:parts, o:o + n]

        rows = [at(0, D), at(D, D)]
        scaled = [at(2 * D, 512), at(2 * D + 512, 512)]
        q_raw, k_raw, q_sq, k_sq, qn, kn, vT, gT, vtok = (at(512 * i, 512) for i in range(9))
        prob = at(4608, TRI)
        probT = at(4608 + TRI, TRI)
        sp_ = at(4608 + 2 * TRI, TRI)
        o_ = 4608 + 3 * TRI
        cl = at(o_, 512, 64)
        cr = at(o_ + 512, 512, 64)
        csum = at(o_ + 1024, 512, PH)
        ftmp = at(4608, 512, PH)
        flog = at(4608 + 512, 512, PH)
        sel = ident[0:PH, 0:PH]
        keysT = at(0, 2 * PH * NKEYS).rearrange("p (j n) -> p j n", n=NKEYS)
        qp = [at(2048, 512), at(2560, 512)]
        s_out = [at(3072, 512), at(3584, 512)]
        gate_piece = at(0, NKEYS * GT)
        s_cur = at(4096, 2048)
        o_ = 6144
        top_v = at(o_, 256).rearrange("p (h c k) -> p h c k", h=PH, c=2)
        top_i = at(o_ + 256, 256).bitcast(U32).rearrange("p (h c k) -> p h c k", h=PH, c=2)
        top_if = at(o_ + 512, 256)
        best = at(o_ + 768, 128)
        pos = at(o_ + 896, 128).bitcast(U32)
        pos2 = at(o_ + 1024, 256).bitcast(U32)
        pos2f = at(o_ + 1280, 256)
        slots = at(o_ + 1536, 384).rearrange("p (a b) -> p a b", a=3)
        slotT = at(o_ + 1920, 384).rearrange("p (a b) -> p a b", a=3)
        gate_lo = at(o_ + 2304, 128)
        gsum = at(o_ + 2432, 16)
        weight = at(o_ + 2448, 128)
        h_out = [at(9216, 512), at(9728, 512)]
        h_grp = at(4096, GRP * T)
        g_grp = at(6144, GRP * T)

        banks = [ctx.enter_context(nc.psum_tensor(f"bank{b}", [P, 512], F32)) for b in range(8)]
        gemm_bank = [banks[4], banks[5]]
        CHUNK_BANKS = [[banks[6], banks[7], banks[4], banks[5]], banks[0:4]]

        score_dram_j = score_dram.rearrange("b p (j n) -> j p b n", n=NKEYS)
        gate_groups = gate_dram.rearrange("c p (g n) -> g p c n", n=GRP * GT)
        act_groups = act_dram.rearrange("(g e) p t -> g p e t", e=GRP)

        x_loaded = sem("x_loaded")
        const_loaded = sem("const_loaded")
        const_base = sem("const_base")
        const_ready = sem("const_ready")
        raw_loaded = [sem(f"raw_loaded{s}") for s in range(2)]
        hi_done = sem("hi_done")
        lo_done = sem("lo_done")
        unit_done = sem("unit_done")
        freed = [sem(f"gemm_freed{s}") for s in range(2)]
        sumsq_done = sem("sumsq_done")
        root_done = sem("root_done")
        inv_done = sem("inv_done")
        row_scaled = sem("row_scaled")
        turned = sem("turned")
        gained = sem("gained")
        xh_done = sem("xh_done")
        xl_done = sem("xl_done")
        act_step = sem("act_step")
        dve_step = sem("dve_step")
        csum_done = sem("csum_done")
        sq_done = sem("sq_done")
        ss_done = sem("ss_done")
        rms_done = sem("rms_done")
        rinv_done = sem("rinv_done")
        qk_normed = sem("qk_normed")
        c_ready = sem("c_ready")
        logits_done = sem("logits_done")
        nmax_done = sem("nmax_done")
        exp_done = sem("exp_done")
        rsum_inv = sem("rsum_inv")
        prob_done = sem("prob_done")
        vt_done = sem("vt_done")
        vtok_done = sem("vtok_done")
        pt_done = sem("pt_done")
        pt_out = sem("pt_out")
        o_done = sem("o_done")
        gate_step = sem("gate_step")
        mixed_done = sem("mixed_done")
        zt_done = sem("zt_done")
        abs_done = sem("abs_done")
        ln_step = sem("ln_step")
        sp_done = sem("sp_done")
        tri_done = sem("tri_done")
        at_done = sem("at_done")
        chunk_done = sem("chunk_done")
        chunk_out = sem("chunk_out")
        keys_loaded = sem("keys_loaded")
        score_done = sem("score_done")
        score_out = sem("score_out")
        score_stored = [sem(f"score_stored{s}") for s in range(2)]
        cur_loaded = sem("cur_loaded")
        topk_step = sem("topk_step")
        diff_done = sem("diff_done")
        gexp_done = sem("gexp_done")
        slots_done = sem("slots_done")
        slots_turned = sem("slots_turned")
        slotT_done = sem("slotT_done")
        hot_a = sem("hot_a")
        hot_b = sem("hot_b")
        gate_done = sem("gate_done")
        gate_out = sem("gate_out")
        gate_stored = sem("gate_stored")
        h_done = sem("h_done")
        h_stored = [sem(f"h_stored{s}") for s in range(2)]
        grp_loaded = sem("grp_loaded")
        w_gated = sem("w_gated")
        w_hi = sem("w_hi")
        w_lo = sem("w_lo")
        y_stored = sem("y_stored")
        mix_hi = sem("mix_hi")
        mix_lo = sem("mix_lo")

        block = ctx.enter_context(nc.Block())

        def load(sp, k, src, i=0, stride=0):
            s = k % 2
            if isinstance(i, int) and k + stride * i < 2:
                pass
            else:
                sp.wait_ge(lo_done, k - 1 + stride * i)
            sp.dma_start(raw[s][:], src).then_inc(raw_loaded[s], 16)

        def split_hi(act, k, i=0, stride=0):
            s = k % 2
            act.wait_ge(raw_loaded[s], 16 * (k // 2 + 1) + 8 * stride * i)
            if not (isinstance(i, int) and k + stride * i < 2):
                act.wait_ge(unit_done, k - 1 + stride * i)
            nc.scalar.activation(wh[s][:], raw[s][:], ACT.Copy).then_inc(hi_done, 1)

        def split_lo(pool, k, i=0, stride=0):
            s = k % 2
            pool.wait_ge(hi_done, k + 1 + stride * i)
            nc.gpsimd.tensor_tensor(wl[s][:], raw[s][:], wh[s][:].bitcast(F32),
                                    ALU.subtract).then_inc(lo_done, 1)

        def gemm(pe, k, m, i=0, stride=0, mstride=0):
            s, b = k % 2, m % 2
            w_h = wh[s][:].rearrange("p (c e) -> p c e", e=P)
            w_l = wl[s][:].rearrange("p (c e) -> p c e", e=P)
            pe.wait_ge(lo_done, k + 1 + stride * i)
            if not (isinstance(i, int) and m + mstride * i < 2):
                pe.wait_ge(freed[b], m // 2 + (mstride // 2) * i)
            for c in range(KC):
                nc.tensor.matmul(gemm_bank[b][:], w_h[:, c], xh[:, c, :], start=(c == 0), stop=False)
                nc.tensor.matmul(gemm_bank[b][:], w_h[:, c], xl[:, c, :], start=False, stop=False)
                last = nc.tensor.matmul(gemm_bank[b][:], w_l[:, c], xh[:, c, :], start=False,
                                        stop=(c == KC - 1))
            last.then_inc(unit_done, 1)

        def chunk_unit(pe, k, odd, first, final, a_hi, a_lo, prev, i=0, stride=0):
            s = k % 2
            w_h = wh[s][:].rearrange("p (e n) -> p e n", e=GRP)
            w_l = wl[s][:].rearrange("p (e n) -> p e n", e=GRP)
            pe.wait_ge(lo_done, k + 1 + stride * i)
            for e in range(GRP):
                for tb in range(TB):
                    bank = CHUNK_BANKS[odd][tb]
                    rows_ = slice(tb * P, tb * P + P)
                    begin = first and e == 0
                    end = final and e == GRP - 1
                    if begin:
                        prev(tb)
                    nc.tensor.matmul(bank[:], a_hi(e)[:, rows_], w_h[:, e], start=begin, stop=False)
                    nc.tensor.matmul(bank[:], a_hi(e)[:, rows_], w_l[:, e], start=False, stop=False)
                    mm = nc.tensor.matmul(bank[:], a_lo(e)[:, rows_], w_h[:, e], start=False, stop=end)
                    if end and tb < TB - 1:
                        mm.then_inc(chunk_done, 1)
            mm.then_inc(unit_done, 1)

        def add_chunk(dve, k, cc, c, odd, i=0, stride=0, cstride=0):
            for tb in range(TB):
                if tb < TB - 1:
                    dve.wait_ge(chunk_done, (TB - 1) * cc + tb + 1 + (TB - 1) * cstride * i)
                else:
                    dve.wait_ge(unit_done, k + 1 + stride * i)
                dst = acc[:, tb, c * 512:(c + 1) * 512] if isinstance(c, int) else \
                    acc[:, tb, bass.ds(c * 512, 512)]
                nc.vector.tensor_tensor(dst, CHUNK_BANKS[odd][tb][:], dst, ALU.add).then_inc(chunk_out, 1)

        def norm_act(act, z):
            for tb in range(TB):
                r = TB * z + tb
                if tb >= 2:
                    act.wait_ge(turned, 16 * z + 4 * (tb - 1))
                nc.scalar.activation(rows[tb % 2], acc[:, tb, :], ACT.Square,
                                     accum_out=stat[:, tb:tb + 1]).then_inc(sumsq_done, 1)
                act.wait_ge(sumsq_done, r + 1)
                nc.scalar.activation(stat[:, 4 + tb:5 + tb], stat[:, tb:tb + 1], ACT.Sqrt,
                                     bias=eps[:, 0:1], scale=1.0 / D).then_inc(root_done, 1)
                if tb:
                    norm_hi(act, z, tb - 1)
            norm_hi(act, z, TB - 1)

        def norm_hi(act, z, tb):
            for a in range(4):
                g = 16 * z + 4 * tb + a
                act.wait_ge(gained, g + 1)
                nc.scalar.activation(xh[:, 4 * a:4 * a + 4, tb * P:(tb + 1) * P],
                                     scaled[g % 2].rearrange("p (c t) -> p c t", c=4),
                                     ACT.Copy).then_inc(xh_done, 1)

        def norm_dve(dve, z):
            for tb in range(TB):
                r = TB * z + tb
                dve.wait_ge(root_done, r + 1)
                nc.vector.reciprocal(stat[:, 8 + tb:9 + tb], stat[:, 4 + tb:5 + tb]).then_inc(inv_done, 1)
                dve.wait_ge(inv_done, r + 1)
                nc.vector.tensor_scalar(rows[tb % 2], acc[:, tb, :], stat[:, 8 + tb:9 + tb], None,
                                        ALU.mult).then_inc(row_scaled, 1)
                for a in range(4):
                    g = 16 * z + 4 * tb + a
                    dve.wait_ge(turned, g + 1)
                    if a >= 2 or tb:
                        dve.wait_ge(xl_done, g - 1)
                    elif z:
                        dve.wait_ge(xl_done, 16 * z)
                    nc.vector.tensor_tensor(
                        scaled[g % 2].rearrange("p (c t) -> p c t", c=4),
                        banks[(4 * tb + a) % 8][:].rearrange("p (c t) -> p c t", c=4),
                        gains[:, z, 4 * a:4 * a + 4].unsqueeze(2).broadcast_to([P, 4, P]),
                        ALU.mult).then_inc(gained, 1)
                    dve.wait_ge(xh_done, g + 1)
                    nc.vector.tensor_tensor(
                        xl[:, 4 * a:4 * a + 4, tb * P:(tb + 1) * P],
                        scaled[g % 2].rearrange("p (c t) -> p c t", c=4),
                        xh[:, 4 * a:4 * a + 4, tb * P:(tb + 1) * P].bitcast(F32),
                        ALU.subtract).then_inc(xl_done, 1)

        def norm_pe(pe, z):
            for tb in range(TB):
                pe.wait_ge(row_scaled, TB * z + tb + 1)
                for a in range(4):
                    g = 16 * z + 4 * tb + a
                    if tb >= 2:
                        pe.wait_ge(gained, g - 7)
                    bank = banks[(4 * tb + a) % 8]
                    for j in range(4):
                        c = 4 * a + j
                        mm = nc.tensor.transpose(bank[:, j * P:(j + 1) * P],
                                                 rows[tb % 2][:, c * P:(c + 1) * P], ident[:])
                    mm.then_inc(turned, 1)

        def n_of(k, i, stride):
            return k + stride * i

        def zero(n):
            return isinstance(n, int) and n <= 0

        def wait_from(eng, s, n):
            if not zero(n):
                eng.wait_ge(s, n)

        def wait_apart(eng, s, n):
            if isinstance(n, int):
                wait_from(eng, s, n)
                return
            eng.wait_ge(s, n)
            own = carry[:, carried[0]:carried[0] + 1]
            carried[0] += 1
            if eng.engine == nc.gpsimd.engine:
                nc.gpsimd.tensor_tensor(own, ones[:, 0:1], ones[:, 0:1], ALU.mult)
            else:
                nc.vector.memset(own, 0.0)

        def evacuated(eng, m, i=0, ms=0):
            eng.wait_ge(freed[m % 2], m // 2 + 1 + (ms // 2) * i)

        def fox_at(buf, i):
            return buf[:, FOX_OFF[i]:FOX_OFF[i + 1]]

        def col_at(buf, j):
            return buf[:, COL_OFF[j]:COL_OFF[j + 1]]

        def mixed_at(h):
            if isinstance(h, int):
                return mixed[:, h * T:(h + 1) * T]
            return mixed[:, bass.ds(h * T, T)]

        @block.sync
        def _(sp):
            for tb in range(TB):
                sp.dma_start(acc[:, tb, :], x[tb * P:(tb + 1) * P, :]).then_inc(x_loaded, 16)
            sp.dma_start(gains[:, 0, :], attn_g).then_inc(const_loaded, 16)
            sp.dma_start(gains[:, 1, :], ffn_g).then_inc(const_loaded, 16)
            sp.dma_start(qk_gain[:, 0:1], q_g).then_inc(const_loaded, 16)
            sp.dma_start(qk_gain[:, 1:2], k_g).then_inc(const_loaded, 16)
            sp.dma_start(bf[:], b_forget).then_inc(const_loaded, 16)
            for n in range(3):
                load(sp, n, w_in[n])
            with sp.Fori(0, (N_OUT - 3) // 2) as i:
                for k in (3, 4):
                    load(sp, k, w_in[i * 2 + k], i, 2)
            load(sp, N_OUT, w_out[0])
            load(sp, N_OUT + 1, w_out[1])
            for tb in range(TB):
                sp.wait_ge(mix_lo, tb + 1)
                sp.dma_start(acc[:, tb, :], x[tb * P:(tb + 1) * P, :]).then_inc(x_loaded, 16)
            with sp.Fori(0, 7) as i:
                for k in (2, 3):
                    load(sp, N_OUT + k, w_out[i * 2 + k], i, 2)
            load(sp, N_PQ, w_pq[0])
            load(sp, N_PQ + 1, w_pq[1])
            sp.wait_ge(xl_done, 32)
            sp.dma_start(keysT, sub_keys).then_inc(keys_loaded, 16)

            def store_scores(j0, i=0):
                j = j0 + 2 * i
                sp.wait_ge(score_out, j + 1)
                sp.dma_start(score_dram_j[j], s_out[j0 % 2].rearrange("p (b n) -> p b n", b=TB)
                             ).then_inc(score_stored[j0 % 2], 16)

            with sp.Fori(0, 7) as i:
                for k in (2, 3):
                    load(sp, N_PQ + k, w_pq[i * 2 + k], i, 2)
                    store_scores(k - 2, i)
            load(sp, N_PRO, u[0])
            store_scores(14)
            load(sp, N_PRO + 1, u[1])
            store_scores(15)

            def store_h(et, m, slot, i=0, ms=0, step=0):
                evacuated(sp, m, i, ms)
                sp.dma_start(act_dram[et], h_out[slot]).then_inc(h_stored[slot], 16)

            def choice_sp(tb):
                for s in range(2):
                    if isinstance(tb, int) and tb == 0:
                        sp.wait_ge(score_stored[s], 16 * PH)
                wait_from(sp, topk_step, tb * TOPK_STEPS)
                sp.dma_start(s_cur, score_dram[tb]).then_inc(cur_loaded, 16)
                for k in range(8):
                    load(sp, N_PRO + k + 2, u[tb * 8 + (k + 2)], tb, 8)
                    store_h(tb * 8 + k, M_PRO + k, k % 2, tb, 8)
                    if k >= 4:
                        q = k - 4
                        sp.wait_ge(gate_out, tb * 32 + 8 * (q + 1))
                        sp.dma_start(gate_dram[tb * 4 + q], gate_piece).then_inc(gate_stored, 16)

            choice_sp(0)
            with sp.Fori(1, TB) as tb:
                choice_sp(tb)

            def load_group(g):
                for s in range(2):
                    sp.wait_ge(h_stored[s], g * 32 + 32)
                sp.dma_start(h_grp.rearrange("p (e t) -> p e t", e=GRP), act_groups[g]).then_inc(grp_loaded, 16)
                sp.dma_start(g_grp.rearrange("p (c n) -> p c n", c=NGC), gate_groups[g]).then_inc(grp_loaded, 16)

            sp.wait_ge(gate_stored, 16 * NGC)
            load_group(0)

            def main_sp(g, last):
                for k in range(8):
                    kk = k + 2
                    if kk < 4:
                        src = u[g * 4 + (GRP * LAG + kk)]
                    elif kk < 8:
                        src = v[g * 4 + (kk - 4)]
                    elif not last:
                        src = u[g * 4 + (GRP * (LAG + 1) + kk - 8)]
                    else:
                        src = v[g * 4 + 4 + (kk - 8)]
                    load(sp, N_MAIN + kk, src, g, 8)
                    if k < 4:
                        store_h(g * 4 + (GRP * LAG + k), M_MAIN + k, k % 2, g, 4)
                    if k == 4:
                        sp.wait_ge(w_lo, g * 4 + 4)
                        load_group(g + 1)

            with sp.Fori(0, NGRP - LAG - 1) as g:
                main_sp(g, False)
            main_sp(NGRP - LAG - 1, True)

            def tail_sp(g, r):
                sp.wait_ge(w_lo, (g + r) * 4 + 4 * (NGRP - LAG) + 4)
                load_group(g + (NGRP - LAG + 1 + r))
                for c in range(CH):
                    load(sp, N_TAIL + 4 * r + c + 2, v[g * 4 + (4 * (NGRP - LAG) + 4 * r + c + 2)], g, 4)

            with sp.Fori(0, 6, 2) as g:
                tail_sp(g, 0)
                tail_sp(g, 1)
            tail_sp(6, 0)
            for c in range(2):
                load(sp, N_TAIL + 28 + c + 2, v[4 * (NGRP - LAG) + 28 + c + 2])
            out_t = out.rearrange("(b p) d -> p b d", p=P)
            for c in range(CH):
                sp.wait_ge(chunk_out, 8 + 4 * (4 * NGRP + c + 1))
                sp.dma_start(out_t[:, :, c * 512:(c + 1) * 512],
                             acc[:, :, c * 512:(c + 1) * 512]).then_inc(y_stored, 16)
            sp.wait_ge(y_stored, 16 * CH)

        @block.gpsimd
        def _(pool):
            nc.gpsimd.memset(ones[:], 1.0)
            nc.gpsimd.memset(neg_ones[:], -1.0)
            nc.gpsimd.memset(ident[:], 0.0)
            nc.gpsimd.memset(fox_mask[:], 0.0)
            nc.gpsimd.memset(eps[:], EPS)
            nc.gpsimd.memset(cl, 0.0)
            nc.gpsimd.memset(cr, 0.0).then_inc(const_base, 1)
            pool.wait_ge(const_base, 1)
            nc.gpsimd.memset(cl[32:40], -1.0)
            nc.gpsimd.memset(cr[0:PH], 1.0).then_inc(const_base, 1)
            pool.wait_ge(const_base, 2)
            nc.gpsimd.iota(iota128[:], [[1, P]], base=0, channel_multiplier=0,
                           allow_small_or_imprecise_dtypes=True)
            nc.gpsimd.iota(iota16[:], [[1, TOPK]], base=0, channel_multiplier=0,
                           allow_small_or_imprecise_dtypes=True)
            nc.gpsimd.affine_select(out=neg_tri[:], in_=neg_ones[:], compare_op=ALU.is_ge, fill=0.0,
                                    base=0, pattern=[[-1, P]], channel_multiplier=1)
            nc.gpsimd.affine_select(out=strict[:], in_=ones[:], compare_op=ALU.is_gt, fill=0.0,
                                    base=0, pattern=[[1, P]], channel_multiplier=-1)
            nc.gpsimd.affine_select(out=sb_mask[:], in_=fox_mask[:], compare_op=ALU.is_gt, fill=MASKED,
                                    base=0, pattern=[[1, P]], channel_multiplier=-1)
            nc.gpsimd.affine_select(out=ident[:], in_=ident[:], compare_op=ALU.not_equal, fill=1.0,
                                    base=0, pattern=[[-1, P]], channel_multiplier=1).then_inc(const_base, 1)
            pool.wait_ge(const_base, 3)
            nc.gpsimd.affine_select(out=fox_mask[:], in_=fox_mask[:], compare_op=ALU.is_ge, fill=MASKED,
                                    base=0, pattern=[[-1, P]], channel_multiplier=1)
            nc.gpsimd.tensor_copy(ident_b[:], ident[:]).then_inc(const_ready, 1)

            with pool.Fori(0, N_PRO // 2) as i:
                split_lo(pool, 0, i, 2)
                split_lo(pool, 1, i, 2)
            split_lo(pool, N_PRO - 1)
            split_lo(pool, N_PRO)

            def choice_pool(tb):
                for k in range(4):
                    split_lo(pool, N_PRO + 1 + k, tb, 8)
                wait_apart(pool, slotT_done, tb + 1)
                for q in range(4):
                    for b in range(8 * q, 8 * q + 8):
                        wait_apart(pool, gate_done, tb * 32 + (b - 1))
                        for t in range(4):
                            o = (b % 2) * 512 + t * P
                            last = nc.gpsimd.tensor_scalar(gh[:, o:o + P], iota128[:],
                                                           slotT[:, 1, 4 * b + t:4 * b + t + 1], None,
                                                           ALU.is_equal)
                        last.then_inc(hot_b, 1)
                    split_lo(pool, N_PRO + 5 + q, tb, 8)

            choice_pool(0)
            with pool.Fori(1, TB) as tb:
                choice_pool(tb)
            with pool.Fori(0, (N_END - N_MAIN - 1) // 2) as i:
                split_lo(pool, N_MAIN + 1, i, 2)
                split_lo(pool, N_MAIN + 2, i, 2)
            if (N_END - N_MAIN - 1) % 2:
                split_lo(pool, N_END - 1)

        @block.scalar
        def _(act):
            act.wait_ge(const_ready, 1)
            act.wait_ge(x_loaded, 16 * TB)
            norm_act(act, 0)
            split_hi(act, 0)

            split_hi(act, 1)

            def forget_act():
                evacuated(act, 0)
                nc.scalar.activation(ftmp, flog, ACT.Abs).then_inc(act_step, 1)
                act.wait_ge(act_step, 1)
                nc.scalar.activation(ftmp, ftmp, ACT.Exp, scale=-1.0).then_inc(act_step, 1)
                act.wait_ge(act_step, 2)
                nc.scalar.activation(ftmp, ftmp, ACT.Ln, bias=ones[0:PH, 0:1]).then_inc(act_step, 1)

            def gate_act(p):
                act.wait_ge(unit_done, p * 4 + 5)
                wait_from(act, mixed_done, p)
                nc.scalar.activation(gT, gemm_bank[0][:], ACT.Exp, scale=-1.0).then_inc(freed[0], 1)

            def exp_act(p):
                wait_from(act, pt_done, p * 4)
                for i in range(TB):
                    act.wait_ge(nmax_done, p * 4 + i + 1)
                    nc.scalar.activation(fox_at(prob, i), banks[i][:, 0:(i + 1) * P], ACT.Exp,
                                         bias=fox_stat[:, i:i + 1],
                                         accum_out=fox_stat[:, 4 + i:5 + i]).then_inc(exp_done, 1)

            def square_act(h, c):
                act.wait_ge(freed[(1 + c) % 2], h * 2 + (1 + c) // 2 + 1)
                wait_from(act, qk_normed, h * 2)
                nc.scalar.activation([q_sq, k_sq][c], [q_raw, k_raw][c], ACT.Square).then_inc(sq_done, 1)

            def value_act(k, i=0, stride=0):
                act.wait_ge(unit_done, k + 1 + stride * i)
                nc.scalar.activation(vT, gemm_bank[k % 2][:], ACT.Copy).then_inc(freed[k % 2], 1)

            def rms_act(h):
                for c, buf in enumerate((q_sq, k_sq)):
                    act.wait_ge(ss_done, h * 2 + c + 1)
                    nc.scalar.activation(buf, banks[c][:], ACT.Sqrt, bias=eps[:, 0:1],
                                         scale=1.0 / HD).then_inc(rms_done, 1)

            def fox_act(h, p):
                if p is not None:
                    gate_act(p)
                split_hi(act, 2, h, 4)
                if p is not None:
                    exp_act(p)
                else:
                    forget_act()
                split_hi(act, 3, h, 4)
                square_act(h, 0)
                split_hi(act, 4, h, 4)
                square_act(h, 1)
                value_act(3, h, 4)
                split_hi(act, 5, h, 4)
                rms_act(h)

            fox_act(0, None)
            fox_act(1, 0)
            with act.Fori(2, NFOX) as h:
                fox_act(h, h - 1)

            def query_act(k, i=0):
                act.wait_ge(unit_done, k + 1 + 6 * i)
                nc.scalar.activation(qn, gemm_bank[k % 2][:], ACT.Copy, scale=SCALE).then_inc(freed[k % 2], 1)

            def softplus_act(s):
                for j in range(TB):
                    act.wait_ge(zt_done, s * 4 + j + 1)
                    nc.scalar.activation(col_at(prob, j), banks[j][:, 0:(TB - j) * P],
                                         ACT.Abs).then_inc(abs_done, 1)
                act.wait_ge(abs_done, s * 4 + 4)
                nc.scalar.activation(prob, prob, ACT.Exp, scale=-1.0).then_inc(ln_step, 1)
                act.wait_ge(ln_step, s * 2 + 1)
                nc.scalar.activation(prob, prob, ACT.Ln, bias=ones[:, 0:1]).then_inc(ln_step, 1)

            def weight_act(s):
                for j in range(TB):
                    act.wait_ge(tri_done, s * 4 + j + 1)
                    nc.scalar.activation(col_at(probT, j), banks[j][:, 0:(TB - j) * P],
                                         ACT.Exp).then_inc(at_done, 1)

            def stick_pair_act(i, peeled):
                for r in range(2):
                    k = N_SB + 3 * r
                    s = i * 2 + r
                    if peeled and r == 0:
                        gate_act(NFOX - 1)
                        split_hi(act, k + 1)
                        exp_act(NFOX - 1)
                        query_act(k)
                        split_hi(act, k + 2)
                        split_hi(act, k + 3)
                    else:
                        value_act(k - 1, i, 6)
                        split_hi(act, k + 1, i, 6)
                        softplus_act(s - 1)
                        query_act(k, i)
                        split_hi(act, k + 2, i, 6)
                        weight_act(s - 1)
                        split_hi(act, k + 3, i, 6)

            stick_pair_act(0, True)
            with act.Fori(1, NSB // 2) as i:
                stick_pair_act(i, False)
            value_act(N_OUT - 1)
            softplus_act(NSB - 1)
            act.wait_ge(unit_done, N_OUT)

            def mix_split(k):
                act.wait_ge(mixed_done, 4 * k + 4)
                nc.scalar.activation(xh[:, 4 * k:4 * k + 4, :].rearrange("p a b -> p (a b)"),
                                     mixed[:, k * D:(k + 1) * D], ACT.Copy).then_inc(mix_hi, 1)

            mix_split(0)
            weight_act(NSB - 1)
            for k in (1, 2, 3):
                mix_split(k)

            with act.Fori(0, N_PQ - N_OUT >> 1) as i:
                split_hi(act, N_OUT + 1, i, 2)
                split_hi(act, N_OUT + 2, i, 2)
            act.wait_ge(chunk_out, 8 + 16)
            norm_act(act, 1)

            def query_out(k, m, i=0):
                act.wait_ge(unit_done, k + 1 + 2 * i)
                nc.scalar.activation(qp[(m - M_PQ) % 2], gemm_bank[m % 2][:],
                                     ACT.Copy).then_inc(freed[m % 2], 1)

            def query_slot(j, i, first):
                if not first:
                    act.wait_ge(score_done, 2 * i + j - 1)
                query_out(N_PQ + j, M_PQ + j, i)

            split_hi(act, N_PQ + 1)
            query_slot(0, 0, True)
            split_hi(act, N_PQ + 2)
            query_slot(1, 0, True)
            with act.Fori(1, PH) as i:
                for j in (0, 1):
                    split_hi(act, N_PQ + j + 1, i, 2)
                    query_slot(j, i, False)

            def gelu_act(k, m, slot, tb, ms, et):
                act.wait_ge(unit_done, k + 1 + (8 * tb))
                wait_from(act, h_stored[slot], et)
                nc.scalar.activation(h_out[slot], gemm_bank[m % 2][:], ACT.Gelu).then_inc(freed[m % 2], 1)

            def choice_act(tb):
                for k in range(4):
                    split_hi(act, N_PRO + k + 1, tb, 8)
                    gelu_act(N_PRO + k, M_PRO + k, k % 2, tb, 8, (tb * 8 + (k - k % 2)) * 8)
                act.wait_ge(diff_done, tb + 1)
                nc.scalar.activation(weight, weight, ACT.Exp).then_inc(gexp_done, 1)
                for q in range(4):
                    wait_from(act, gate_stored, (tb * 4 + q) * 16)
                    for b in range(8 * q, 8 * q + 8):
                        act.wait_ge(gate_done, tb * 32 + b + 1)
                        nc.scalar.activation(
                            gate_piece.rearrange("p (i t) -> p t i", t=GT)[:, 4 * (b % 8):4 * (b % 8) + 4],
                            banks[6 + b % 2][:].rearrange("p (t i) -> p t i", t=4),
                            ACT.Copy).then_inc(gate_out, 1)
                    k = 4 + q
                    split_hi(act, N_PRO + k + 1, tb, 8)
                    gelu_act(N_PRO + k, M_PRO + k, k % 2, tb, 8, (tb * 8 + (k - k % 2)) * 8)

            choice_act(0)
            with act.Fori(1, TB) as tb:
                choice_act(tb)

            def main_act(g):
                for k in range(8):
                    if 1 <= k <= 4:
                        gelu_act(N_MAIN + k - 1, M_MAIN + k - 1, (k - 1) % 2, g, 4,
                                 g * 32 + 8 * (GRP * LAG + (k - 1 - (k - 1) % 2)))
                    split_hi(act, N_MAIN + k + 1, g, 8)
                    if k < 4:
                        act.wait_ge(w_gated, g * 4 + k + 1)
                        if k == 0:
                            act.wait_ge(unit_done, g * 8 + N_MAIN)
                        nc.scalar.activation(gh[:, k * T:(k + 1) * T], h_grp[:, k * T:(k + 1) * T],
                                             ACT.Copy).then_inc(w_hi, 1)

            with act.Fori(0, NGRP - LAG) as g:
                main_act(g)

            def tail_w_act(g, r, first=False):
                if not first:
                    act.wait_ge(unit_done, g * 4 + (N_TAIL + 4 * (r - 1)))
                for j in range(GRP):
                    act.wait_ge(w_gated, (g + (NGRP - LAG + r)) * 4 + j + 1)
                    nc.scalar.activation(xh[:, 4 * (r % 2) + j, :], h_grp[:, j * T:(j + 1) * T],
                                         ACT.Copy).then_inc(w_hi, 1)

            act.wait_ge(unit_done, N_TAIL - 4)
            tail_w_act(0, 0, True)

            def tail_act(g, r, last=False):
                for c in range(CH):
                    if not (last and c == CH - 1):
                        split_hi(act, N_TAIL + 4 * r + c + 1, g, 4)
                    if c == 0 and not last:
                        tail_w_act(g, r + 1)

            with act.Fori(0, 6, 2) as g:
                tail_act(g, 0)
                tail_act(g, 1)
            tail_act(6, 0)
            tail_act(6, 1, last=True)

        @block.vector
        def _(dve):
            dve.wait_ge(const_ready, 1)
            dve.wait_ge(const_loaded, 16 * 5)
            dve.wait_ge(x_loaded, 16 * TB)
            nc.vector.tensor_scalar(qk_gain[:, 2:3], qk_gain[:, 0:1], SCALE, None, ALU.mult)
            norm_dve(dve, 0)

            def copy_out(k, dst, i=0, stride=0):
                dve.wait_ge(unit_done, k + 1 + stride * i)
                nc.vector.tensor_copy(dst, gemm_bank[k % 2][:]).then_inc(freed[k % 2], 1)

            def max_dve(p):
                for i in range(TB):
                    dve.wait_ge(logits_done, p * 4 + i + 1)
                    nc.vector.tensor_reduce(fox_stat[:, i:i + 1], banks[i][:, 0:(i + 1) * P], AX.X, ALU.max,
                                            negate=True).then_inc(nmax_done, 1)

            def prob_dve(p):
                for i in range(TB):
                    dve.wait_ge(exp_done, p * 4 + i + 1)
                    nc.vector.reciprocal(fox_stat[:, 8 + i:9 + i],
                                         fox_stat[:, 4 + i:5 + i]).then_inc(rsum_inv, 1)
                for i in range(TB):
                    dve.wait_ge(rsum_inv, p * 4 + i + 1)
                    nc.vector.tensor_scalar(fox_at(prob, i), fox_at(prob, i), fox_stat[:, 8 + i:9 + i],
                                            None, ALU.mult).then_inc(prob_done, 1)

            def vtok_dve(a):
                dve.wait_ge(vt_done, a + 1)
                nc.vector.tensor_copy(vtok, banks[7][:]).then_inc(vtok_done, 1)

            def turned_dve(p):
                for j in range(TB):
                    dve.wait_ge(pt_done, p * 4 + j + 1)
                    nc.vector.tensor_copy(col_at(probT, j), banks[j][:, 0:(TB - j) * P]).then_inc(pt_out, 1)

            def gate_dve(p):
                dve.wait_ge(freed[0], p * 2 + 3)
                nc.vector.tensor_scalar(gT, gT, 1.0, None, ALU.add).then_inc(gate_step, 1)
                dve.wait_ge(gate_step, p * 2 + 1)
                nc.vector.reciprocal(gT, gT).then_inc(gate_step, 1)
                dve.wait_ge(gate_step, p * 2 + 2)
                dve.wait_ge(o_done, p + 1)
                nc.vector.tensor_tensor(mixed_at(p), banks[6][:], gT, ALU.mult).then_inc(mixed_done, 1)

            def decay_dve(h):
                wait_from(dve, logits_done, h * 4)
                pick = sel[:, h:h + 1] if isinstance(h, int) else sel[:, bass.ds(h, 1)]
                nc.vector.tensor_scalar(cl[0:PH], csum, pick, None, ALU.mult)
                nc.vector.tensor_scalar(cr[32:32 + PH], csum, pick, None, ALU.mult).then_inc(c_ready, 1)

            def rms_dve(h):
                for c, buf in enumerate((q_sq, k_sq)):
                    dve.wait_ge(rms_done, h * 2 + c + 1)
                    nc.vector.reciprocal(buf, buf).then_inc(rinv_done, 1)
                for c, (buf, src, dst) in enumerate(((q_sq, q_raw, qn), (k_sq, k_raw, kn))):
                    dve.wait_ge(rinv_done, h * 2 + c + 1)
                    nc.vector.scalar_tensor_tensor(out=dst, in0=src, scalar=qk_gain[:, 2 - c:3 - c], in1=buf,
                                                   op0=ALU.mult, op1=ALU.mult).then_inc(qk_normed, 1)

            def fox_dve(h, p):
                if p is not None:
                    max_dve(p)
                    prob_dve(p)
                else:
                    dve.wait_ge(unit_done, 1)
                    nc.vector.tensor_scalar(flog, gemm_bank[0][0:PH, :], bf[:, 0:1], None,
                                            ALU.add).then_inc(freed[0], 1)
                copy_out(1, q_raw, h, 4)
                if p is not None:
                    vtok_dve(p)
                copy_out(2, k_raw, h, 4)
                if p is not None:
                    turned_dve(p)
                    gate_dve(p)
                else:
                    dve.wait_ge(act_step, 3)
                    nc.vector.scalar_tensor_tensor(out=flog, in0=flog, scalar=0.0, in1=ftmp, op0=ALU.min,
                                                   op1=ALU.subtract).then_inc(dve_step, 1)
                    dve.wait_ge(dve_step, 1)
                    nc.vector.tensor_tensor_scan(csum, cr[0:PH], flog, 0.0, ALU.mult,
                                                 ALU.add).then_inc(csum_done, 1)
                    dve.wait_ge(csum_done, 1)
                decay_dve(h)
                rms_dve(h)

            fox_dve(0, None)
            fox_dve(1, 0)
            with dve.Fori(2, NFOX) as h:
                fox_dve(h, h - 1)

            def softplus_dve(s):
                dve.wait_ge(ln_step, s * 2 + 2)
                for j in range(TB):
                    nc.vector.scalar_tensor_tensor(out=col_at(sp_, j), in0=banks[j][:, 0:(TB - j) * P],
                                                   scalar=0.0, in1=col_at(prob, j), op0=ALU.max,
                                                   op1=ALU.add).then_inc(sp_done, 1)
                for j in range(TB):
                    dve.wait_ge(sp_done, s * 8 + j + 1)
                    diag = col_at(sp_, j)[:, 0:P]
                    nc.vector.tensor_tensor(diag, diag, strict[:], ALU.mult).then_inc(sp_done, 1)

            def mixed_dve(s):
                dve.wait_ge(o_done, s + (NFOX + 1))
                nc.vector.tensor_copy(mixed_at(s + NFOX), banks[6][:]).then_inc(mixed_done, 1)

            def stick_pair_dve(i, peeled):
                for r in range(2):
                    k = N_SB + 3 * r
                    s = i * 2 + r
                    if peeled and r == 0:
                        max_dve(NFOX - 1)
                        prob_dve(NFOX - 1)
                        vtok_dve(NFOX - 1)
                        turned_dve(NFOX - 1)
                        copy_out(k + 1, kn)
                        gate_dve(NFOX - 1)
                    else:
                        softplus_dve(s - 1)
                        vtok_dve(s + (NFOX - 1))
                        copy_out(k + 1, kn, i, 6)
                        mixed_dve(s - 1)

            stick_pair_dve(0, True)
            with dve.Fori(1, NSB // 2) as i:
                stick_pair_dve(i, False)
            softplus_dve(NSB - 1)
            vtok_dve(HEADS - 1)

            def mix_rest(k):
                dve.wait_ge(mix_hi, k + 1)
                nc.vector.tensor_tensor(xl[:, 4 * k:4 * k + 4, :].rearrange("p a b -> p (a b)"),
                                        mixed[:, k * D:(k + 1) * D],
                                        xh[:, 4 * k:4 * k + 4, :].rearrange("p a b -> p (a b)").bitcast(F32),
                                        ALU.subtract).then_inc(mix_lo, 1)

            mix_rest(0)
            mixed_dve(NSB - 1)
            nc.vector.memset(stat[:, 12:13], 0.0).then_inc(chunk_out, 8)
            for k in (1, 2, 3):
                mix_rest(k)

            dve.wait_ge(x_loaded, 2 * 16 * TB)
            with dve.Fori(0, 2) as w:
                for r in range(2):
                    add_chunk(dve, N_OUT + 4 * r + 3, r, w * 2 + r, r, w, 8, 2)
            dve.wait_ge(chunk_out, 8 + 16)
            norm_dve(dve, 1)

            def score_out_dve(j, i=0):
                dve.wait_ge(score_done, i * 2 + j + 1)
                if not isinstance(i, int):
                    dve.wait_ge(score_stored[j], i * 16)
                nc.vector.tensor_copy(s_out[j], banks[j][:]).then_inc(score_out, 1)

            score_out_dve(0)
            score_out_dve(1)
            with dve.Fori(1, PH) as i:
                score_out_dve(0, i)
                score_out_dve(1, i)

            def choice_dve(tb):
                count = [0]

                def step(ins):
                    count[0] += 1
                    ins.then_inc(topk_step, 1)
                    wait_apart(dve, topk_step, tb * TOPK_STEPS + count[0])

                halves = [(h, c) for h in range(PH) for c in range(2)]

                def s_of(h, c):
                    return s_cur[:, (2 * h + c) * NKEYS:(2 * h + c + 1) * NKEYS]

                wait_apart(dve, cur_loaded, tb * 16 + 16)
                for r in range(2):
                    e = slice(8 * r, 8 * r + 8)
                    for h, c in halves:
                        last = nc.vector.max(top_v[:, h, c, e], s_of(h, c))
                    step(last)
                    for h, c in halves:
                        last = nc.vector.max_index(top_i[:, h, c, e], top_v[:, h, c, e], s_of(h, c))
                    step(last)
                    if r == 0:
                        for h, c in halves:
                            last = nc.vector.match_replace(s_of(h, c), top_v[:, h, c, e], s_of(h, c), LOWEST)
                        step(last)
                cand = s_cur.rearrange("p (h a b) -> p h a b", h=PH, a=TOPK)
                cand_of = [s_cur[:, 256 * h:256 * h + 256] for h in range(PH)]
                best_h = best.rearrange("p (h k) -> p h k", h=PH)
                weight_h = weight.rearrange("p (h k) -> p h k", h=PH)
                pos_h = pos.rearrange("p (h k) -> p h k", h=PH)
                step(nc.vector.tensor_tensor(cand, top_v[:, :, 0, :].unsqueeze(3).broadcast_to([P, PH, TOPK, TOPK]),
                                             top_v[:, :, 1, :].unsqueeze(2).broadcast_to([P, PH, TOPK, TOPK]),
                                             ALU.add))
                for r in range(2):
                    e = slice(8 * r, 8 * r + 8)
                    for h in range(PH):
                        last = nc.vector.max(best_h[:, h, e], cand_of[h])
                    step(last)
                    for h in range(PH):
                        last = nc.vector.max_index(pos_h[:, h, e], best_h[:, h, e], cand_of[h])
                    step(last)
                    if r == 0:
                        for h in range(PH):
                            last = nc.vector.match_replace(cand_of[h], best_h[:, h, e], cand_of[h], LOWEST)
                        step(last)
                nc.vector.tensor_tensor(weight_h, best_h, best_h[:, :, 0:1].broadcast_to([P, PH, TOPK]),
                                        ALU.subtract).then_inc(diff_done, 1)
                nc.vector.tensor_scalar(pos2[:, 0:128], pos, 4, None, ALU.logical_shift_right)
                nc.vector.tensor_scalar(pos2[:, 128:256], pos, 15, None, ALU.bitwise_and)
                step(nc.vector.tensor_copy(top_if, top_i.rearrange("p h c k -> p (h c k)")))
                step(nc.vector.tensor_copy(pos2f, pos2))
                look = s_cur.rearrange("p (h k j) -> p h k j", h=PH, k=TOPK)
                look_s = s_cur.rearrange("p (s j) -> p s j", j=TOPK)
                idx_f = top_if.rearrange("p (h c k) -> p h c k", h=PH, c=2)
                for c in range(2):
                    step(nc.vector.tensor_tensor(
                        look_s, pos2f[:, 128 * c:128 * c + 128].unsqueeze(2).broadcast_to([P, P, TOPK]),
                        iota16[:].unsqueeze(1).broadcast_to([P, P, TOPK]), ALU.is_equal))
                    step(nc.vector.tensor_tensor(
                        look, look, idx_f[:, :, c, :].unsqueeze(2).broadcast_to([P, PH, TOPK, TOPK]), ALU.mult))
                    step(nc.vector.tensor_reduce(slots[:, c, :], look_s, AX.X, ALU.add))
                dve.wait_ge(gexp_done, tb + 1)
                step(nc.vector.tensor_reduce(gsum[:, 0:PH], weight_h, AX.X, ALU.add))
                step(nc.vector.reciprocal(gsum[:, PH:2 * PH], gsum[:, 0:PH]))
                nc.vector.tensor_tensor(slots[:, 2, :].rearrange("p (h k) -> p h k", h=PH), weight_h,
                                        gsum[:, PH:2 * PH].unsqueeze(2).broadcast_to([P, PH, TOPK]),
                                        ALU.mult).then_inc(slots_done, 1)
                dve.wait_ge(slots_turned, tb + 1)
                step(nc.vector.tensor_copy(slotT.rearrange("p a b -> p (a b)"), banks[0][:, 0:3 * P]))
                step(nc.vector.tensor_copy(gate_hi[:], slotT[:, 2, :]))
                nc.vector.tensor_tensor(gate_lo, slotT[:, 2, :], gate_hi[:].bitcast(F32),
                                        ALU.subtract).then_inc(slotT_done, 1)
                dve.wait_ge(slotT_done, tb + 1)
                for b in range(32):
                    wait_from(dve, gate_done, tb * 32 + (b - 1))
                    for t in range(4):
                        o = (b % 2) * 512 + t * P
                        n = 4 * b + t
                        nc.vector.tensor_scalar(gh[:, 1024 + o:1024 + o + P], iota128[:],
                                                slotT[:, 0, n:n + 1], gate_hi[:, n:n + 1].bitcast(F32),
                                                ALU.is_equal, ALU.mult)
                        last = nc.vector.tensor_scalar(gl[:, o:o + P], iota128[:],
                                                       slotT[:, 0, n:n + 1], gate_lo[:, n:n + 1],
                                                       ALU.is_equal, ALU.mult)
                    last.then_inc(hot_a, 1)
                assert count[0] == TOPK_STEPS, count[0]

            choice_dve(0)
            with dve.Fori(1, TB) as tb:
                choice_dve(tb)

            def gate_group(g, hi_of, lo_of):
                dve.wait_ge(grp_loaded, g * 32 + 32)
                for j in range(GRP):
                    mine = h_grp[:, j * T:(j + 1) * T].rearrange("p (c t) -> p c t", c=NGC)
                    nc.vector.tensor_tensor(
                        mine, mine, g_grp.rearrange("p (c e t) -> p c e t", c=NGC, e=GRP)[:, :, j, :],
                        ALU.mult).then_inc(w_gated, 1)
                for j in range(GRP):
                    dve.wait_ge(w_hi, g * 4 + j + 1)
                    nc.vector.tensor_tensor(lo_of(j), h_grp[:, j * T:(j + 1) * T], hi_of(j).bitcast(F32),
                                            ALU.subtract).then_inc(w_lo, 1)

            with dve.Fori(0, NGRP - LAG) as g:
                gate_group(g, lambda j: gh[:, j * T:(j + 1) * T], lambda j: gl[:, j * T:(j + 1) * T])
                for c in range(CH):
                    add_chunk(dve, N_MAIN + GRP + c, 4 + c, c, c % 2, g, 8, 4)

            def tail_w_dve(g, r):
                b = 4 * (r % 2)
                gate_group(g + (NGRP - LAG + r), lambda j: xh[:, b + j, :], lambda j: xl[:, b + j, :])

            def tail_dve(g, r, last=False):
                if not last:
                    tail_w_dve(g, r + 1)
                for c in range(CH):
                    add_chunk(dve, N_TAIL + 4 * r + c, 4 + 4 * (NGRP - LAG + r) + c, c, c % 2, g, 4, 4)

            tail_w_dve(0, 0)
            with dve.Fori(0, 6, 2) as g:
                tail_dve(g, 0)
                tail_dve(g, 1)
            tail_dve(6, 0)
            tail_dve(6, 1, last=True)

        @block.tensor
        def _(pe):
            pe.wait_ge(const_ready, 1)
            norm_pe(pe, 0)
            pe.wait_ge(xl_done, 16)
            gemm(pe, 0, 0)

            def sumsq_pe(h):
                for c, buf in enumerate((q_sq, k_sq)):
                    pe.wait_ge(sq_done, h * 2 + c + 1)
                    if c == 0:
                        wait_from(pe, pt_out, h * 4)
                    nc.tensor.matmul(banks[c][:], ones[:], buf, start=True, stop=True).then_inc(ss_done, 1)

            def logits_pe(p):
                pe.wait_ge(qk_normed, p * 2 + 2)
                pe.wait_ge(c_ready, p + 1)
                for i in range(TB):
                    n = (i + 1) * P
                    qs = slice(i * P, n)
                    nc.tensor.matmul(banks[i][:, 0:n], qn[:, qs], kn[:, 0:n], start=True, stop=False)
                    nc.tensor.matmul(banks[i][:, 0:n], cl[0:32 + PH, qs], cr[0:32 + PH, 0:n],
                                     start=False, stop=False)
                    nc.tensor.matmul(banks[i][:, qs], ident_b[:], fox_mask[:], start=False,
                                     stop=True).then_inc(logits_done, 1)

            def vturn_pe(a, k, i=0, stride=0):
                evacuated(pe, k, i, stride)
                wait_from(pe, vtok_done, a)
                for j in range(TB):
                    mm = nc.tensor.transpose(banks[7][:, j * P:(j + 1) * P], vT[:, j * P:(j + 1) * P], ident[:])
                mm.then_inc(vt_done, 1)

            def pturn_pe(p):
                pe.wait_ge(prob_done, p * 4 + 4)
                for j in range(TB):
                    for i in range(j, TB):
                        mm = nc.tensor.transpose(banks[j][:, (i - j) * P:(i - j + 1) * P],
                                                 fox_at(prob, i)[:, j * P:(j + 1) * P], ident[:])
                    mm.then_inc(pt_done, 1)

            def out_pe(a, ready, n):
                pe.wait_ge(ready, n)
                pe.wait_ge(vtok_done, a + 1)
                wait_from(pe, mixed_done, a)
                for j in range(TB):
                    mm = nc.tensor.matmul(banks[6][:, j * P:T], vtok[:, j * P:(j + 1) * P], col_at(probT, j),
                                          start=(j == 0), stop=(j == TB - 1))
                mm.then_inc(o_done, 1)

            def fox_pe(h, p):
                if p is not None:
                    logits_pe(p)
                gemm(pe, 1, 1, h, 4, 4)
                if p is not None:
                    vturn_pe(p, 3, p, 4)
                gemm(pe, 2, 2, h, 4, 4)
                if p is not None:
                    pturn_pe(p)
                gemm(pe, 3, 3, h, 4, 4)
                if p is not None:
                    out_pe(p, pt_out, p * 4 + 4)
                sumsq_pe(h)
                gemm(pe, 4, 4, h, 4, 4)

            fox_pe(0, None)
            fox_pe(1, 0)
            with pe.Fori(2, NFOX) as h:
                fox_pe(h, h - 1)

            def z_pe(s, k, i=0):
                evacuated(pe, k, i, 6)
                evacuated(pe, k + 1, i, 6)
                if isinstance(s, int) and s == 0:
                    pe.wait_ge(pt_out, 4 * NFOX)
                else:
                    pe.wait_ge(at_done, s * 4)
                for j in range(TB):
                    nc.tensor.matmul(banks[j][:, 0:(TB - j) * P], kn[:, j * P:(j + 1) * P], qn[:, j * P:T],
                                     start=True, stop=True).then_inc(zt_done, 1)

            def tri_pe(s):
                pe.wait_ge(sp_done, s * 8 + 8)
                for j in range(TB):
                    nc.tensor.matmul(banks[j][:, 0:(TB - j) * P], neg_tri[:], col_at(sp_, j), start=False,
                                     stop=False, skip_group_check=True)
                    for l in range(j + 1, TB):
                        nc.tensor.matmul(banks[j][:, (l - j) * P:(TB - j) * P], neg_ones[:], col_at(sp_, l),
                                         start=False, stop=False, skip_group_check=True)
                    nc.tensor.matmul(banks[j][:, 0:P], ident_b[:], sb_mask[:], start=False, stop=True,
                                     skip_group_check=True).then_inc(tri_done, 1)

            def stick_pair_pe(i, peeled):
                for r in range(2):
                    k = N_SB + 3 * r
                    s = i * 2 + r
                    if peeled and r == 0:
                        logits_pe(NFOX - 1)
                        gemm(pe, k, k)
                        vturn_pe(NFOX - 1, 3, NFOX - 1, 4)
                        pturn_pe(NFOX - 1)
                        gemm(pe, k + 1, k + 1)
                        out_pe(NFOX - 1, pt_out, 4 * NFOX)
                        gemm(pe, k + 2, k + 2)
                    else:
                        z_pe(s - 1, k - 3, i)
                        gemm(pe, k, k, i, 6, 6)
                        vturn_pe(s + (NFOX - 1), k - 1, i, 6)
                        tri_pe(s - 1)
                        gemm(pe, k + 1, k + 1, i, 6, 6)
                        out_pe(s + (NFOX - 1), at_done, s * 4)
                        gemm(pe, k + 2, k + 2, i, 6, 6)

            stick_pair_pe(0, True)
            with pe.Fori(1, NSB // 2) as i:
                stick_pair_pe(i, False)
            z_pe(NSB - 1, N_OUT - 3)
            vturn_pe(HEADS - 1, N_OUT - 1)
            tri_pe(NSB - 1)
            out_pe(HEADS - 1, at_done, 4 * NSB)

            with pe.Fori(0, 2) as w:
                for r in range(2):
                    for q in range(4):
                        pe.wait_ge(mix_lo, q + 1)
                        chunk_unit(pe, N_OUT + 4 * r + q, r, q == 0, q == 3,
                                   lambda e: xh[:, 4 * q + e, :], lambda e: xl[:, 4 * q + e, :],
                                   lambda tb: pe.wait_ge(chunk_out, w * 8 + 4 * r + tb + 1), w, 8)
            norm_pe(pe, 1)
            pe.wait_ge(xl_done, 32)

            def score_pe(j, i=0):
                evacuated(pe, M_PQ + j, i, 2)
                if not isinstance(i, int):
                    pe.wait_ge(score_out, i * 2 + (j - 1))
                b = j % 2
                for tb in range(TB):
                    n = i * 2 + j
                    mm = nc.tensor.matmul(banks[b][:, tb * P:(tb + 1) * P], qp[b][:, tb * P:(tb + 1) * P],
                                          keysT[:, n, :], start=True, stop=True)
                mm.then_inc(score_done, 1)

            gemm(pe, N_PQ, M_PQ)
            pe.wait_ge(keys_loaded, 16)
            score_pe(0)
            gemm(pe, N_PQ + 1, M_PQ + 1)
            score_pe(1)
            with pe.Fori(1, PH) as i:
                for j in range(2):
                    gemm(pe, N_PQ + j, M_PQ + j, i, 2, 2)
                    score_pe(j, i)

            def choice_pe(tb):
                for k in range(4):
                    gemm(pe, N_PRO + k, M_PRO + k, tb, 8, 8)
                pe.wait_ge(slots_done, tb + 1)
                for a in range(3):
                    mm = nc.tensor.transpose(banks[0][:, a * P:(a + 1) * P], slots[:, a, :], ident[:])
                mm.then_inc(slots_turned, 1)
                for q in range(4):
                    for b in range(8 * q, 8 * q + 8):
                        pe.wait_ge(hot_a, tb * 32 + b + 1)
                        pe.wait_ge(hot_b, tb * 32 + b + 1)
                        wait_from(pe, gate_out, tb * 32 + (b - 1))
                        for t in range(4):
                            o = (b % 2) * 512 + t * P
                            dst = banks[6 + b % 2][:, t * P:(t + 1) * P]
                            nc.tensor.matmul(dst, gh[:, o:o + P], gh[:, 1024 + o:1024 + o + P],
                                             start=True, stop=False)
                            mm = nc.tensor.matmul(dst, gh[:, o:o + P], gl[:, o:o + P], start=False, stop=True)
                        mm.then_inc(gate_done, 1)
                    gemm(pe, N_PRO + 4 + q, M_PRO + 4 + q, tb, 8, 8)

            choice_pe(0)
            with pe.Fori(1, TB) as tb:
                choice_pe(tb)
            pe.wait_ge(gate_out, TB * 32)

            with pe.Fori(0, NGRP - LAG) as g:
                for k in range(GRP):
                    m = M_MAIN + k
                    if k < 2:
                        pe.wait_ge(chunk_out, g * 16 + 17 + (2 + m % 2))
                    gemm(pe, N_MAIN + k, m, g, 8, 4)
                for c in range(CH):
                    def bank_free(tb):
                        pe.wait_ge(chunk_out, g * 16 + 16 + 4 * c + tb + 1)
                        if c == 0 and tb >= 2:
                            evacuated(pe, M_MAIN + (3 if tb == 2 else 2), g, 4)
                    if c == 0:
                        pe.wait_ge(w_lo, g * 4 + 4)
                    chunk_unit(pe, N_MAIN + GRP + c, c % 2, True, True,
                               lambda e: gh[:, e * T:(e + 1) * T], lambda e: gl[:, e * T:(e + 1) * T],
                               bank_free, g, 8)

            def tail_pe(g, r):
                pe.wait_ge(w_lo, (g + (NGRP - LAG + r)) * 4 + 4)
                for c in range(CH):
                    base = 4 * (4 + 4 * (NGRP - LAG + r) + c)
                    chunk_unit(pe, N_TAIL + 4 * r + c, c % 2, True, True,
                               lambda e: xh[:, 4 * r + e, :], lambda e: xl[:, 4 * r + e, :],
                               lambda tb: pe.wait_ge(chunk_out, g * 16 + base + tb + 1), g, 4)

            with pe.Fori(0, 8, 2) as g:
                tail_pe(g, 0)
                tail_pe(g, 1)


_INS = ["x", "attn_g", "w_in", "b_forget", "q_g", "k_g", "w_out", "ffn_g", "w_pq", "sub_keys", "u", "v"]


def kernel(x, attn_norm_g, w_in, b_forget, q_norm_g, k_norm_g, w_out, ffn_norm_g, w_peer_q,
           peer_sub_keys, peer_u, peer_v):
    import numpy as np
    import concourse.bacc as bacc
    from concourse.bass_utils import run_bass_kernel_spmd

    def arr(a):
        return np.asarray(a)

    def units(w):
        return np.ascontiguousarray(w.reshape(KC, P, -1, P).transpose(2, 1, 0, 3)).reshape(-1, P, D)

    wi = arr(w_in)[0]
    d1 = NFOX * HD
    cols = [np.arange(7 * d1, 7 * d1 + PH), np.arange(P - PH)]
    for h in range(NFOX):
        cols += [np.arange(s * d1 + h * HD, s * d1 + (h + 1) * HD) for s in range(4)]
    for h in range(NSB):
        cols += [np.arange((4 + s) * d1 + h * HD, (4 + s) * d1 + (h + 1) * HD) for s in range(3)]
    data = {
        "x": arr(x)[0],
        "attn_g": np.ascontiguousarray(arr(attn_norm_g)[0].reshape(KC, P).T),
        "w_in": units(wi[:, np.concatenate(cols)]),
        "b_forget": arr(b_forget)[0].reshape(PH, 1),
        "q_g": arr(q_norm_g)[0].reshape(P, 1),
        "k_g": arr(k_norm_g)[0].reshape(P, 1),
        "w_out": np.ascontiguousarray(arr(w_out)[0].reshape(4, 4, P, CH, 512).transpose(3, 0, 2, 1, 4)
                                      ).reshape(-1, P, D),
        "ffn_g": np.ascontiguousarray(arr(ffn_norm_g)[0].reshape(KC, P).T),
        "w_pq": units(arr(w_peer_q)[0]),
        "sub_keys": np.ascontiguousarray(arr(peer_sub_keys)[0].reshape(2 * PH, NKEYS, P).transpose(2, 0, 1)),
        "u": np.ascontiguousarray(arr(peer_u)[0].reshape(NKEYS, P, KC, P).transpose(0, 3, 2, 1)
                                  ).reshape(NKEYS, P, D),
        "v": np.ascontiguousarray(arr(peer_v)[0].reshape(NGRP, GRP, P, CH, 512).transpose(0, 3, 2, 1, 4)
                                  ).reshape(-1, P, D),
    }
    nc = bacc.Bacc("TRN2", target_bir_lowering=False, num_devices=1)
    args, arrays = [], {}
    for name in _INS:
        a = np.ascontiguousarray(data[name])
        arrays[f"in_{name}"] = a
        args.append(nc.dram_tensor(f"in_{name}", a.shape, mybir.dt.from_np(a.dtype), kind="ExternalInput").ap())
    args.append(nc.dram_tensor("out_y", (T, D), F32, kind="ExternalOutput").ap())
    build(nc, *args)
    nc.compile()
    r = run_bass_kernel_spmd(nc, [arrays], core_ids=[0])
    return r.results[0]["out_y"].reshape(1, T, D)
```

```python
from contextlib import ExitStack

import concourse.bass as bass
from concourse import mybir

F32 = mybir.dt.float32
F32R = mybir.dt.float32r
BF16 = mybir.dt.bfloat16
U32 = mybir.dt.uint32
ALU = mybir.AluOpType
ACT = mybir.ActivationFunctionType
AX = mybir.AxisListType

P = 128
T = 512
D = 2048
TB = T // P
KC = D // P
HD = 128
NFOX = 8
NSB = 8
HEADS = NFOX + NSB
PH = 8
TOPK = 16
NKEYS = 128
GRP = 4
NGRP = NKEYS // GRP
CH = D // 512
LAG = 9
DB = TB - 1
TD = DB * P
NMAIN = NGRP - LAG
GT = 32
NGC = TD // GT
SLOTS = PH * TOPK
TILES0, TILES = 6, 10
GM = 5
GTAIL = (2, 1)
G_TAIL0 = GM * NMAIN
EPS = 1e-6
SCALE = float(HD) ** -0.5
LOWEST = -3.0e38
MASKED = -1.0e30

N_FOX = 1
N_SB = N_FOX + 4 * NFOX
N_OUT = N_SB + 3 * NSB
N_PQ = N_OUT + CH * (HEADS // 4)
N_PRO = N_PQ + 2 * PH
N_MAIN = N_PRO + GRP * LAG
N_TAIL = N_MAIN + 2 * GRP * NMAIN
N_END = N_TAIL + GRP * LAG
assert TILES0 + DB * TILES == GRP * LAG
assert G_TAIL0 + (LAG // 2) * sum(GTAIL) + 1 == SLOTS
M_PQ = N_OUT
M_PRO = M_PQ + 2 * PH
M_MAIN = M_PRO + GRP * LAG

MAIN_BUF = (0, 1, 2, 0, 1, 2, 0, 1, 2, 1)
TAIL_BUF = (0, 1, 2, 0, 1, 2)
MAIN_BACK = (4, 2, 4, 3, 3, 3, 3, 3, 3, 2)
TAIL_BACK = (3, 2, 3, 3, 3, 3)
TICKETS = 4

TOPK_STEPS = 21

FOX_OFF = [P * i * (i + 1) // 2 for i in range(TB + 1)]
COL_OFF = [0]
for _j in range(TB):
    COL_OFF.append(COL_OFF[-1] + P * (TB - _j))
TRI = FOX_OFF[TB]


def build(nc, x, attn_g, w_in, b_forget, q_g, k_g, w_out, ffn_g, ffn_row, w_pq, sub_keys, u, v, u_rows,
          v_rows, out):
    ctx = ExitStack()
    with ctx:
        def sb(name, shape, dt=F32):
            return ctx.enter_context(nc.sbuf_tensor(name, shape, dt))

        def sem(name):
            return ctx.enter_context(nc.semaphore(name))

        score_dram = nc.dram_tensor("score_scratch", [TB, P, 2 * PH * NKEYS], F32, kind="Internal").ap()
        gate_dram = nc.dram_tensor("gate_scratch", [NGC, P, NKEYS * GT], F32, kind="Internal").ap()
        act_dram = nc.dram_tensor("act_scratch", [NKEYS, P, TD], F32, kind="Internal").ap()

        acc = sb("acc", [P, TB, D])
        mixed = acc[:].rearrange("p a b -> p (a b)")
        xh = sb("xh", [P, KC, T], F32R)
        xl = sb("xl", [P, KC, T], F32R)
        raw = [sb(f"raw{s}", [P, D]) for s in range(2)]
        wh = [sb(f"wh{s}", [P, D], F32R) for s in range(2)]
        wl = [sb(f"wl{s}", [P, D], F32R) for s in range(2)]
        gh = sb("gh", [P, GRP * TD], F32R)
        gl = sb("gl", [P, GRP * TD], F32R)

        ident = sb("ident", [P, P])
        ones = sb("ones", [P, P])
        iota128 = sb("iota128", [P, P])
        iota16 = sb("iota16", [P, TOPK])
        gains = sb("gains", [P, 2, KC])
        qk_gain = sb("qk_gain", [P, 3])
        bf = sb("bf", [PH, 1])
        eps = sb("eps", [P, 1])
        stat = sb("stat", [P, 16])
        carry = sb("carry", [P, 80])
        g_idx = sb("g_idx", [P, SLOTS], U32)
        g_wt = sb("g_wt", [P, SLOTS])
        idx_u = sb("idx_u", [P, GM], U32)
        idx_v = sb("idx_v", [P, GM], U32)
        dots = sb("dots", [P, 2 * GM])
        carried = [0]

        arena = sb("arena", [P, 12432])

        def at(o, n, parts=P):
            return arena[0:parts, o:o + n]

        rows = [at(0, D), at(D, D)]
        scaled = [at(2 * D, 512), at(2 * D + 512, 512)]
        gain_row = at(5120, D)
        squares = at(7168, 1024).bitcast(BF16)
        x_tok = at(9616, D)
        q_raw, k_raw, q_sq, k_sq, qn, kn, vT, gT, vtok = (at(512 * i, 512) for i in range(9))
        prob = at(4608, TRI)
        probT = at(4608 + TRI, TRI)
        sp_ = at(4608 + 2 * TRI, TRI)
        o_ = 4608 + 3 * TRI
        cl = at(o_, 512, 64)
        cr = at(o_ + 512, 512, 64)
        csum = at(o_ + 1024, 512, PH)
        neg_ones = at(9984, P)
        neg_tri = at(9984 + P, P)
        strict = at(9984 + 2 * P, P)
        o_ = 9984 + 3 * P
        ident_b = at(o_, P // 2).bitcast(BF16)
        fox_mask = at(o_ + P // 2, P // 2).bitcast(BF16)
        sb_mask = at(o_ + P, P // 2).bitcast(BF16)
        fox_stat = at(o_ + 3 * P // 2, 16)
        ftmp = at(4608, 512, PH)
        flog = at(4608 + 512, 512, PH)
        sel = ident[0:PH, 0:PH]
        keysT = at(0, 2 * PH * NKEYS).rearrange("p (j n) -> p j n", n=NKEYS)
        qp = [at(2048, 512), at(2560, 512)]
        s_out = [at(3072, 512), at(3584, 512)]
        gate_piece = at(0, NKEYS * GT)
        s_cur = at(4096, 2048)
        o_ = 6144
        top_v = at(o_, 256).rearrange("p (h c k) -> p h c k", h=PH, c=2)
        top_i = at(o_ + 256, 256).bitcast(U32).rearrange("p (h c k) -> p h c k", h=PH, c=2)
        top_if = at(o_ + 512, 256)
        best = at(o_ + 768, 128)
        pos = at(o_ + 896, 128).bitcast(U32)
        pos2 = at(o_ + 1024, 256).bitcast(U32)
        pos2f = at(o_ + 1280, 256)
        slots = at(o_ + 1536, 384).rearrange("p (a b) -> p a b", a=3)
        slotT = at(o_ + 1920, 384).rearrange("p (a b) -> p a b", a=3)
        gsum = at(o_ + 2304, 16)
        weight = at(o_ + 2320, 128)
        h_out = [at(9616 + D, TD), at(9616 + D + TD, TD)]
        hot_gate = [at(8592, 512), at(8592 + 512, 512)]
        rows_g = [at(0, D), at(D, D), at(4096 + 2 * GRP * TD, D)]
        h_grp = at(4096, GRP * TD)
        g_grp = at(4096 + GRP * TD, GRP * TD)

        banks = [ctx.enter_context(nc.psum_tensor(f"bank{b}", [P, 512], F32)) for b in range(8)]
        gemm_bank = [banks[4], banks[5]]
        CHUNK_BANKS = [[banks[6], banks[7], banks[4], banks[5]], banks[0:4]]
        GATE_BANKS = [banks[6], banks[7], banks[3], banks[1]]
        DENSE_BANKS = [[banks[6], banks[7], banks[3]], banks[0:3]]

        score_dram_j = score_dram.rearrange("b p (j n) -> j p b n", n=NKEYS)
        gate_groups = gate_dram.rearrange("c p (g n) -> g p c n", n=GRP * GT)
        act_groups = act_dram.rearrange("(g e) p t -> g p e t", e=GRP)

        x_loaded = sem("x_loaded")
        const_loaded = sem("const_loaded")
        const_base = sem("const_base")
        const_ready = sem("const_ready")
        raw_loaded = [sem(f"raw_loaded{s}") for s in range(2)]
        hi_done = sem("hi_done")
        lo_done = sem("lo_done")
        unit_done = sem("unit_done")
        freed = [sem(f"gemm_freed{s}") for s in range(2)]
        sumsq_done = sem("sumsq_done")
        root_done = sem("root_done")
        inv_done = sem("inv_done")
        row_scaled = sem("row_scaled")
        turned = sem("turned")
        gained = sem("gained")
        xh_done = sem("xh_done")
        xl_done = sem("xl_done")
        act_step = sem("act_step")
        dve_step = sem("dve_step")
        csum_done = sem("csum_done")
        sq_done = sem("sq_done")
        ss_done = sem("ss_done")
        rms_done = sem("rms_done")
        rinv_done = sem("rinv_done")
        qk_normed = sem("qk_normed")
        c_ready = sem("c_ready")
        logits_done = sem("logits_done")
        nmax_done = sem("nmax_done")
        exp_done = sem("exp_done")
        rsum_inv = sem("rsum_inv")
        prob_done = sem("prob_done")
        vt_done = sem("vt_done")
        vtok_done = sem("vtok_done")
        pt_done = sem("pt_done")
        pt_out = sem("pt_out")
        o_done = sem("o_done")
        gate_step = sem("gate_step")
        mixed_done = sem("mixed_done")
        zt_done = sem("zt_done")
        abs_done = sem("abs_done")
        ln_step = sem("ln_step")
        sp_done = sem("sp_done")
        tri_done = sem("tri_done")
        at_done = sem("at_done")
        chunk_done = sem("chunk_done")
        chunk_out = sem("chunk_out")
        keys_loaded = sem("keys_loaded")
        score_done = sem("score_done")
        score_out = sem("score_out")
        score_stored = [sem(f"score_stored{s}") for s in range(2)]
        cur_loaded = sem("cur_loaded")
        topk_step = sem("topk_step")
        diff_done = sem("diff_done")
        gexp_done = sem("gexp_done")
        slots_done = sem("slots_done")
        slots_turned = sem("slots_turned")
        slotT_done = sem("slotT_done")
        hot_done = sem("hot_done")
        gate_done = sem("gate_done")
        gate_out = sem("gate_out")
        gate_stored = sem("gate_stored")
        h_done = sem("h_done")
        h_stored = [sem(f"h_stored{s}") for s in range(2)]
        grp_loaded = sem("grp_loaded")
        w_gated = sem("w_gated")
        w_hi = sem("w_hi")
        w_lo = sem("w_lo")
        y_stored = sem("y_stored")
        xtok_done = sem("xtok_done")
        chosen_done = sem("chosen_done")
        gwt_done = sem("gwt_done")
        idx_u_ready = sem("idx_u_ready")
        idx_v_ready = sem("idx_v_ready")
        gathered = [sem(f"gathered{b}") for b in range(3)]
        gather_used = sem("gather_used")
        dots_act = sem("dots_act")
        coef_done = sem("coef_done")
        mix_hi = sem("mix_hi")
        mix_lo = sem("mix_lo")

        block = ctx.enter_context(nc.Block())

        def load(sp, k, src, i=0, stride=0):
            s = k % 2
            if isinstance(i, int) and k + stride * i < 2:
                pass
            else:
                sp.wait_ge(lo_done, k - 1 + stride * i)
            sp.dma_start(raw[s][:], src).then_inc(raw_loaded[s], 16)

        def split_hi(act, k, i=0, stride=0):
            s = k % 2
            act.wait_ge(raw_loaded[s], 16 * (k // 2 + 1) + 8 * stride * i)
            if not (isinstance(i, int) and k + stride * i < 2):
                act.wait_ge(unit_done, k - 1 + stride * i)
            nc.scalar.activation(wh[s][:], raw[s][:], ACT.Copy).then_inc(hi_done, 1)

        def split_lo(pool, k, i=0, stride=0):
            s = k % 2
            pool.wait_ge(hi_done, k + 1 + stride * i)
            nc.gpsimd.tensor_tensor(wl[s][:], raw[s][:], wh[s][:].bitcast(F32),
                                    ALU.subtract).then_inc(lo_done, 1)

        def gemm(pe, k, m, i=0, stride=0, mstride=0, width=T, between=None):
            s, b = k % 2, m % 2
            w_h = wh[s][:].rearrange("p (c e) -> p c e", e=P)
            w_l = wl[s][:].rearrange("p (c e) -> p c e", e=P)
            pe.wait_ge(lo_done, k + 1 + stride * i)
            if not (isinstance(i, int) and m + mstride * i < 2):
                pe.wait_ge(freed[b], m // 2 + (mstride // 2) * i)
            dst = gemm_bank[b][:, 0:width]
            for c in range(KC):
                nc.tensor.matmul(dst, w_h[:, c], xh[:, c, 0:width], start=(c == 0), stop=False)
                nc.tensor.matmul(dst, w_h[:, c], xl[:, c, 0:width], start=False, stop=False)
                last = nc.tensor.matmul(dst, w_l[:, c], xh[:, c, 0:width], start=False,
                                        stop=(c == KC - 1))
                if c == KC - 1:
                    last.then_inc(unit_done, 1)
                if between is not None and c % 2 == 1:
                    between(c // 2)

        def chunk_unit(pe, k, set_, first, final, a_hi, a_lo, prev, i=0, stride=0):
            s = k % 2
            w_h = wh[s][:].rearrange("p (e n) -> p e n", e=GRP)
            w_l = wl[s][:].rearrange("p (e n) -> p e n", e=GRP)
            pe.wait_ge(lo_done, k + 1 + stride * i)
            for e in range(GRP):
                for tb, bank in enumerate(set_):
                    rows_ = slice(tb * P, tb * P + P)
                    begin = first and e == 0
                    end = final and e == GRP - 1
                    if begin:
                        prev(tb)
                    nc.tensor.matmul(bank[:], a_hi(e)[:, rows_], w_h[:, e], start=begin, stop=False)
                    nc.tensor.matmul(bank[:], a_hi(e)[:, rows_], w_l[:, e], start=False, stop=False)
                    mm = nc.tensor.matmul(bank[:], a_lo(e)[:, rows_], w_h[:, e], start=False, stop=end)
                    if end and tb < len(set_) - 1:
                        mm.then_inc(chunk_done, 1)
            mm.then_inc(unit_done, 1)

        def add_chunk(dve, k, done, c, set_, i=0, stride=0, dstride=0):
            for tb, bank in enumerate(set_):
                if tb < len(set_) - 1:
                    dve.wait_ge(chunk_done, done + tb + 1 + dstride * i)
                else:
                    dve.wait_ge(unit_done, k + 1 + stride * i)
                dst = acc[:, tb, c * 512:(c + 1) * 512] if isinstance(c, int) else \
                    acc[:, tb, bass.ds(c * 512, 512)]
                nc.vector.tensor_tensor(dst, bank[:], dst, ALU.add).then_inc(chunk_out, 1)

        def norm_act(act, z):
            def root(tb):
                r = TB * z + tb
                if z == 0:
                    act.wait_ge(x_loaded, 16 * TB)
                if r:
                    act.wait_ge(sumsq_done, r)
                nc.scalar.activation(squares, acc[:, tb, :], ACT.Square,
                                     accum_out=stat[:, tb:tb + 1]).then_inc(sumsq_done, 1)
                act.wait_ge(sumsq_done, r + 1)
                nc.scalar.activation(stat[:, 4 + tb:5 + tb], stat[:, tb:tb + 1], ACT.Sqrt,
                                     bias=eps[:, 0:1], scale=1.0 / D).then_inc(root_done, 1)

            for tb in range(TB - 1):
                root(tb)
            norm_hi(act, z, 0)
            root(TB - 1)
            for tb in range(1, TB):
                norm_hi(act, z, tb)
                if z == 0 and tb < 3:
                    split_hi(act, tb - 1)

        def norm_hi(act, z, tb):
            for a in range(4):
                g = 16 * z + 4 * tb + a
                act.wait_ge(gained, g + 1)
                nc.scalar.activation(xh[:, 4 * a:4 * a + 4, tb * P:(tb + 1) * P],
                                     scaled[g % 2].rearrange("p (c t) -> p c t", c=4),
                                     ACT.Copy).then_inc(xh_done, 1)

        def norm_dve(dve, z):
            def scale_rows(tb):
                r = TB * z + tb
                dve.wait_ge(root_done, r + 1)
                nc.vector.reciprocal(stat[:, 8 + tb:9 + tb], stat[:, 4 + tb:5 + tb]).then_inc(inv_done, 1)
                dve.wait_ge(inv_done, r + 1)
                if tb >= 2:
                    dve.wait_ge(turned, 16 * z + 4 * (tb - 1))
                nc.vector.tensor_scalar(rows[tb % 2], acc[:, tb, :], stat[:, 8 + tb:9 + tb], None,
                                        ALU.mult).then_inc(row_scaled, 1)

            def gain(n):
                g = 16 * z + n
                dve.wait_ge(turned, g + 1)
                if g >= 2:
                    dve.wait_ge(xl_done, g - 1)
                nc.vector.tensor_tensor(
                    scaled[g % 2].rearrange("p (c t) -> p c t", c=4),
                    banks[n % 8][:].rearrange("p (c t) -> p c t", c=4),
                    gains[:, z, 4 * (n % 4):4 * (n % 4) + 4].unsqueeze(2).broadcast_to([P, 4, P]),
                    ALU.mult).then_inc(gained, 1)

            def rest(n):
                g, a, tb = 16 * z + n, n % 4, n // 4
                dve.wait_ge(xh_done, g + 1)
                nc.vector.tensor_tensor(
                    xl[:, 4 * a:4 * a + 4, tb * P:(tb + 1) * P],
                    scaled[g % 2].rearrange("p (c t) -> p c t", c=4),
                    xh[:, 4 * a:4 * a + 4, tb * P:(tb + 1) * P].bitcast(F32),
                    ALU.subtract).then_inc(xl_done, 1)

            scale_rows(0)
            scale_rows(1)
            gain(0)
            for n in range(16):
                if n < 15:
                    gain(n + 1)
                rest(n)
                if n in (1, 5):
                    scale_rows(n // 4 + 2)

        def norm_pe(pe, z):
            for tb in range(TB):
                pe.wait_ge(row_scaled, TB * z + tb + 1)
                for a in range(4):
                    g = 16 * z + 4 * tb + a
                    if tb >= 2:
                        pe.wait_ge(gained, g - 7)
                    bank = banks[(4 * tb + a) % 8]
                    for j in range(4):
                        c = 4 * a + j
                        mm = nc.tensor.transpose(bank[:, j * P:(j + 1) * P],
                                                 rows[tb % 2][:, c * P:(c + 1) * P], ident[:])
                    mm.then_inc(turned, 1)

        def zero(n):
            return isinstance(n, int) and n <= 0

        def in_main(j, g=0, ahead=0):
            b = MAIN_BUF[j]
            per = MAIN_BUF.count(b)
            return (g * len(MAIN_BUF) + (len(MAIN_BUF) * ahead + j), b,
                    g * per + (per * ahead + MAIN_BUF[:j].count(b) + 1), MAIN_BACK[j])

        def in_tail(j, i=0, ahead=0):
            b = TAIL_BUF[j]
            per = TAIL_BUF.count(b)
            return (i * len(TAIL_BUF) + (2 * G_TAIL0 + len(TAIL_BUF) * ahead + j), b,
                    i * per + (MAIN_BUF.count(b) * NMAIN + per * ahead + TAIL_BUF[:j].count(b) + 1), TAIL_BACK[j])

        def wait_from(eng, s, n):
            if not zero(n):
                eng.wait_ge(s, n)

        def wait_apart(eng, s, n):
            if isinstance(n, int):
                wait_from(eng, s, n)
                return
            eng.wait_ge(s, n)
            own = carry[:, carried[0]:carried[0] + 1]
            carried[0] += 1
            if eng.engine == nc.gpsimd.engine:
                nc.gpsimd.tensor_tensor(own, ones[:, 0:1], ones[:, 0:1], ALU.mult)
            else:
                nc.vector.memset(own, 0.0)

        def evacuated(eng, m, i=0, ms=0):
            eng.wait_ge(freed[m % 2], m // 2 + 1 + (ms // 2) * i)

        def fox_at(buf, i):
            return buf[:, FOX_OFF[i]:FOX_OFF[i + 1]]

        def col_at(buf, j):
            return buf[:, COL_OFF[j]:COL_OFF[j + 1]]

        def mixed_at(h):
            if isinstance(h, int):
                return mixed[:, h * T:(h + 1) * T]
            return mixed[:, bass.ds(h * T, T)]

        @block.sync
        def _(sp):
            for tb in range(TB):
                sp.dma_start(acc[:, tb, :], x[tb * P:(tb + 1) * P, :]).then_inc(x_loaded, 16)
            sp.dma_start(gains[:, 0, :], attn_g).then_inc(const_loaded, 16)
            sp.dma_start(gains[:, 1, :], ffn_g).then_inc(const_loaded, 16)
            sp.dma_start(qk_gain[:, 0:1], q_g).then_inc(const_loaded, 16)
            sp.dma_start(qk_gain[:, 1:2], k_g).then_inc(const_loaded, 16)
            sp.dma_start(bf[:], b_forget).then_inc(const_loaded, 16)
            for n in range(3):
                load(sp, n, w_in[n])
            with sp.Fori(0, (N_OUT - 3) // 2) as i:
                for k in (3, 4):
                    load(sp, k, w_in[i * 2 + k], i, 2)
            load(sp, N_OUT, w_out[0])
            load(sp, N_OUT + 1, w_out[1])
            load(sp, N_OUT + 2, w_out[2])
            load(sp, N_OUT + 3, w_out[3])
            for tb in range(TB):
                sp.wait_ge(mix_lo, tb + 1)
                sp.dma_start(acc[:, tb, :], x[tb * P:(tb + 1) * P, :]).then_inc(x_loaded, 16)
            sp.dma_start(gain_row, ffn_row.partition_broadcast(P)).then_inc(const_loaded, 16)
            with sp.Fori(0, 6) as i:
                for k in (4, 5):
                    load(sp, N_OUT + k, w_out[i * 2 + k], i, 2)
            load(sp, N_PQ, w_pq[0])
            load(sp, N_PQ + 1, w_pq[1])
            sp.wait_ge(xl_done, 32)
            sp.dma_start(keysT, sub_keys).then_inc(keys_loaded, 16)

            def store_scores(j0, i=0):
                j = j0 + 2 * i
                sp.wait_ge(score_out, j + 1)
                sp.dma_start(score_dram_j[j], s_out[j0 % 2].rearrange("p (b n) -> p b n", b=TB)
                             ).then_inc(score_stored[j0 % 2], 16)

            load(sp, N_PQ + 2, w_pq[2])
            with sp.Fori(0, 6) as i:
                for k in (3, 4):
                    load(sp, N_PQ + k, w_pq[i * 2 + k], i, 2)
                    store_scores(k - 3, i)
            load(sp, N_PQ + 15, w_pq[15])
            store_scores(12)
            load(sp, N_PRO, u[0])
            store_scores(13)
            load(sp, N_PRO + 1, u[1])
            store_scores(14)
            store_scores(15)

            def store_h(et, m, slot, i=0, ms=0):
                evacuated(sp, m, i, ms)
                sp.dma_start(act_dram[et], h_out[slot]).then_inc(h_stored[slot], 16)

            for s in range(2):
                sp.wait_ge(score_stored[s], 16 * PH)
            sp.sem_inc(gate_stored, 16)
            for s in range(2):
                sp.sem_inc(h_stored[s], 16)
            sp.sem_inc(gather_used, TICKETS)
            sp.wait_ge(xtok_done, 1)
            sp.dma_start(s_cur, score_dram[TB - 1]).then_inc(cur_loaded, 16)
            for k in range(TILES0):
                load(sp, N_PRO + k + 2, u[k + 2])
                if k:
                    store_h(k - 1, M_PRO + k - 1, (k - 1) % 2)

            sp.wait_ge(topk_step, TOPK_STEPS)
            sp.dma_start(s_cur, score_dram[0]).then_inc(cur_loaded, 16)
            with sp.Fori(0, DB) as t:
                for j in range(TILES):
                    k = TILES0 + j
                    load(sp, N_PRO + k + 2, u[t * TILES + (k + 2)], t, TILES)
                    if j == TILES - 4:
                        sp.wait_ge(topk_step, t * TOPK_STEPS + 2 * TOPK_STEPS)
                        sp.dma_start(s_cur, score_dram[t + 1]).then_inc(cur_loaded, 16)
                    store_h(t * TILES + (k - 1), M_PRO + k - 1, (k - 1) % 2, t, TILES)
                    if j >= TILES - 4:
                        q = j - (TILES - 4)
                        sp.wait_ge(gate_out, t * 32 + (8 * q + 8 + len(GATE_BANKS)))
                        sp.dma_start(gate_dram[t * 4 + q], gate_piece).then_inc(gate_stored, 16)
            k = TILES0 + DB * TILES - 1
            store_h(k, M_PRO + k, k % 2)

            def load_acts(g):
                for s in range(2):
                    sp.wait_ge(h_stored[s], g * 32 + 48)
                sp.dma_start(h_grp.rearrange("p (e t) -> p e t", e=GRP), act_groups[g]).then_inc(grp_loaded, 16)

            def load_gates(g):
                sp.dma_start(g_grp.rearrange("p (c n) -> p c n", c=NGC), gate_groups[g]).then_inc(grp_loaded, 16)

            def load_group(g):
                load_acts(g)
                load_gates(g)

            sp.wait_ge(gate_stored, 16 * NGC + 16)
            sp.wait_ge(chosen_done, 1 + DB)
            sp.wait_ge(cur_loaded, 16 * (2 + DB))
            load_group(0)

            def main_sp(g, last):
                for k in range(8):
                    kk = k + 2
                    if kk < 4:
                        src = u[g * 4 + (GRP * LAG + kk)]
                    elif kk < 8:
                        src = v[g * 4 + (kk - 4)]
                    elif not last:
                        src = u[g * 4 + (GRP * (LAG + 1) + kk - 8)]
                    else:
                        src = v[g * 4 + 4 + (kk - 8)]
                    load(sp, N_MAIN + kk, src, g, 8)
                    if 1 <= k <= 4:
                        store_h(g * 4 + (GRP * LAG + k - 1), M_MAIN + k - 1, (k - 1) % 2, g, 4)
                    if k == 4:
                        sp.wait_ge(w_lo, g * 4 + 4)
                        load_acts(g + 1)
                    if k == 5:
                        load_gates(g + 1)

            with sp.Fori(0, NMAIN - 1) as g:
                main_sp(g, False)
            main_sp(NMAIN - 1, True)

            def tail_sp(i, r):
                sp.wait_ge(w_lo, i * 8 + 4 * (NMAIN + r + 1))
                load_group(i * 2 + (NMAIN + 1 + r))
                for c in range(CH):
                    load(sp, N_TAIL + 4 * r + c + 2, v[i * 8 + (4 * NMAIN + 4 * r + c + 2)], i, 8)

            with sp.Fori(0, LAG // 2) as i:
                tail_sp(i, 0)
                tail_sp(i, 1)
            for n in range(2, CH):
                load(sp, N_END - CH + n, v[CH * NGRP - CH + n])
            out_t = out.rearrange("(b p) d -> p b d", p=P)
            for c in range(CH):
                sp.wait_ge(chunk_out, 24 + 3 * (4 * (NGRP - 1) + c + 1))
                sp.dma_start(out_t[:, 0:DB, c * 512:(c + 1) * 512],
                             acc[:, 0:DB, c * 512:(c + 1) * 512]).then_inc(y_stored, 16)
            sp.wait_ge(gather_used, TICKETS + 2 * SLOTS)
            sp.dma_start(out_t[:, DB, :], acc[:, DB, :]).then_inc(y_stored, 16)
            sp.wait_ge(y_stored, 16 * (CH + 1))

        @block.gpsimd
        def _(pool):
            nc.gpsimd.memset(ones[:], 1.0)
            nc.gpsimd.memset(neg_ones, -1.0)
            nc.gpsimd.memset(ident[:], 0.0)
            nc.gpsimd.memset(fox_mask, 0.0)
            nc.gpsimd.memset(eps[:], EPS)
            nc.gpsimd.memset(cl, 0.0)
            nc.gpsimd.memset(cr, 0.0).then_inc(const_base, 1)
            pool.wait_ge(const_base, 1)
            nc.gpsimd.memset(cl[32:40], -1.0)
            nc.gpsimd.memset(cr[0:PH], 1.0).then_inc(const_base, 1)
            pool.wait_ge(const_base, 2)
            nc.gpsimd.iota(iota128[:], [[1, P]], base=0, channel_multiplier=0,
                           allow_small_or_imprecise_dtypes=True)
            nc.gpsimd.iota(iota16[:], [[1, TOPK]], base=0, channel_multiplier=0,
                           allow_small_or_imprecise_dtypes=True)
            nc.gpsimd.affine_select(out=neg_tri, in_=neg_ones, compare_op=ALU.is_ge, fill=0.0,
                                    base=0, pattern=[[-1, P]], channel_multiplier=1)
            nc.gpsimd.affine_select(out=strict, in_=ones[:], compare_op=ALU.is_gt, fill=0.0,
                                    base=0, pattern=[[1, P]], channel_multiplier=-1)
            nc.gpsimd.affine_select(out=sb_mask, in_=fox_mask, compare_op=ALU.is_gt, fill=MASKED,
                                    base=0, pattern=[[1, P]], channel_multiplier=-1)
            nc.gpsimd.affine_select(out=ident[:], in_=ident[:], compare_op=ALU.not_equal, fill=1.0,
                                    base=0, pattern=[[-1, P]], channel_multiplier=1).then_inc(const_base, 1)
            pool.wait_ge(const_base, 3)
            nc.gpsimd.affine_select(out=fox_mask, in_=fox_mask, compare_op=ALU.is_ge, fill=MASKED,
                                    base=0, pattern=[[-1, P]], channel_multiplier=1)
            nc.gpsimd.tensor_copy(ident_b, ident[:]).then_inc(const_ready, 1)

            with pool.Fori(0, N_PRO // 2) as i:
                split_lo(pool, 0, i, 2)
                split_lo(pool, 1, i, 2)
            split_lo(pool, N_PRO - 1)
            split_lo(pool, N_PRO)

            with pool.Fori(0, (N_MAIN - N_PRO) // 2) as i:
                split_lo(pool, N_PRO + 1, i, 2)
                split_lo(pool, N_PRO + 2, i, 2)

            def gather(table, idx, j, place):
                q, b, _, back = place
                wait_apart(pool, gather_used, q + (TICKETS + 1 - back))
                nc.gpsimd.indirect_dma_start(
                    out=rows_g[b], out_offset=None, in_=table,
                    in_offset=bass.IndirectOffsetOnAxis(ap=idx[:, j:j + 1], axis=0)
                ).then_inc(gathered[b], 16)

            def group_gathers(ns, place, grp):
                def issue(j):
                    if j == 0:
                        wait_apart(pool, idx_u_ready, grp + 1)
                    if j == ns:
                        wait_apart(pool, idx_v_ready, grp + 1)
                    gather(u_rows if j < ns else v_rows, idx_u if j < ns else idx_v, j % ns, place(j))
                return issue

            pool.wait_ge(gate_stored, 16 * NGC + 16)
            first = group_gathers(GM, in_main, 0)
            first(0)

            def main_pool(g, nxt):
                mine = group_gathers(GM, lambda j: in_main(j, g), g)
                for k in range(8):
                    split_lo(pool, N_MAIN + k + 1, g, 8)
                    for j in ((1, 2), (3,), (4,), (5, 6), (7,), (8,), (9,), ())[k]:
                        mine(j)
                nxt(0)

            with pool.Fori(0, NMAIN - 1) as g:
                main_pool(g, group_gathers(GM, lambda j: in_main(j, g, 1), g + 1))
            main_pool(NMAIN - 1, group_gathers(GTAIL[0], in_tail, NMAIN))

            def tail_pool(i, nxt):
                even = group_gathers(GTAIL[0], lambda j: in_tail(j, i), i * 2 + NMAIN)
                odd = group_gathers(GTAIL[1], lambda j: in_tail(4 + j, i), i * 2 + (NMAIN + 1))
                for c in range(CH):
                    split_lo(pool, N_TAIL + c + 1, i, 8)
                    if c < CH - 1:
                        even(c + 1)
                odd(0)
                split_lo(pool, N_TAIL + CH + 1, i, 8)
                odd(1)
                for c in range(1, CH):
                    split_lo(pool, N_TAIL + CH + c + 1, i, 8)
                nxt(0)

            with pool.Fori(0, LAG // 2 - 1) as i:
                tail_pool(i, group_gathers(GTAIL[0], lambda j: in_tail(j, i, 1), i * 2 + (NMAIN + 2)))
            final = group_gathers(1, lambda j: in_tail(j, LAG // 2), NGRP - 1)
            tail_pool(LAG // 2 - 1, final)
            split_lo(pool, N_END - 3)
            final(1)
            split_lo(pool, N_END - 2)
            split_lo(pool, N_END - 1)

        @block.scalar
        def _(act):
            act.wait_ge(const_ready, 1)
            act.wait_ge(x_loaded, 16 * TB)
            norm_act(act, 0)

            def forget_act():
                evacuated(act, 0)
                nc.scalar.activation(ftmp, flog, ACT.Abs).then_inc(act_step, 1)
                act.wait_ge(act_step, 1)
                nc.scalar.activation(ftmp, ftmp, ACT.Exp, scale=-1.0).then_inc(act_step, 1)
                act.wait_ge(act_step, 2)
                nc.scalar.activation(ftmp, ftmp, ACT.Ln, bias=ones[0:PH, 0:1]).then_inc(act_step, 1)

            def gate_act(p):
                act.wait_ge(unit_done, p * 4 + 5)
                wait_from(act, mixed_done, p)
                nc.scalar.activation(gT, gemm_bank[0][:], ACT.Exp, scale=-1.0).then_inc(freed[0], 1)

            def exp_act(p):
                wait_from(act, pt_done, p * 4)
                for i in range(TB):
                    act.wait_ge(nmax_done, p * 4 + i + 1)
                    nc.scalar.activation(fox_at(prob, i), banks[i][:, 0:(i + 1) * P], ACT.Exp,
                                         bias=fox_stat[:, i:i + 1],
                                         accum_out=fox_stat[:, 4 + i:5 + i]).then_inc(exp_done, 1)

            def square_act(h, c):
                act.wait_ge(freed[(1 + c) % 2], h * 2 + (1 + c) // 2 + 1)
                wait_from(act, qk_normed, h * 2)
                nc.scalar.activation([q_sq, k_sq][c], [q_raw, k_raw][c], ACT.Square).then_inc(sq_done, 1)

            def value_act(k, i=0, stride=0):
                act.wait_ge(unit_done, k + 1 + stride * i)
                nc.scalar.activation(vT, gemm_bank[k % 2][:], ACT.Copy).then_inc(freed[k % 2], 1)

            def rms_act(h):
                for c, buf in enumerate((q_sq, k_sq)):
                    act.wait_ge(ss_done, h * 2 + c + 1)
                    nc.scalar.activation(buf, banks[c][:], ACT.Sqrt, bias=eps[:, 0:1],
                                         scale=1.0 / HD).then_inc(rms_done, 1)

            def fox_act(h, p):
                if p is not None:
                    gate_act(p)
                split_hi(act, 2, h, 4)
                if p is not None:
                    exp_act(p)
                else:
                    forget_act()
                split_hi(act, 3, h, 4)
                square_act(h, 0)
                split_hi(act, 4, h, 4)
                square_act(h, 1)
                value_act(3, h, 4)
                split_hi(act, 5, h, 4)
                rms_act(h)

            fox_act(0, None)
            fox_act(1, 0)
            with act.Fori(2, NFOX) as h:
                fox_act(h, h - 1)

            def query_act(k, i=0):
                act.wait_ge(unit_done, k + 1 + 6 * i)
                nc.scalar.activation(qn, gemm_bank[k % 2][:], ACT.Copy, scale=SCALE).then_inc(freed[k % 2], 1)

            def softplus_act(s):
                for j in range(TB):
                    act.wait_ge(zt_done, s * 4 + j + 1)
                    nc.scalar.activation(col_at(prob, j), banks[j][:, 0:(TB - j) * P],
                                         ACT.Abs).then_inc(abs_done, 1)
                act.wait_ge(abs_done, s * 4 + 4)
                nc.scalar.activation(prob, prob, ACT.Exp, scale=-1.0).then_inc(ln_step, 1)
                act.wait_ge(ln_step, s * 2 + 1)
                nc.scalar.activation(prob, prob, ACT.Ln, bias=ones[:, 0:1]).then_inc(ln_step, 1)

            def weight_act(s):
                for j in range(TB):
                    act.wait_ge(tri_done, s * 4 + j + 1)
                    nc.scalar.activation(col_at(probT, j), banks[j][:, 0:(TB - j) * P],
                                         ACT.Exp).then_inc(at_done, 1)

            def stick_pair_act(i, peeled):
                for r in range(2):
                    k = N_SB + 3 * r
                    s = i * 2 + r
                    if peeled and r == 0:
                        gate_act(NFOX - 1)
                        split_hi(act, k + 1)
                        exp_act(NFOX - 1)
                        query_act(k)
                        split_hi(act, k + 2)
                        split_hi(act, k + 3)
                    else:
                        value_act(k - 1, i, 6)
                        split_hi(act, k + 1, i, 6)
                        softplus_act(s - 1)
                        query_act(k, i)
                        split_hi(act, k + 2, i, 6)
                        weight_act(s - 1)
                        split_hi(act, k + 3, i, 6)

            stick_pair_act(0, True)
            with act.Fori(1, NSB // 2) as i:
                stick_pair_act(i, False)
            value_act(N_OUT - 1)
            softplus_act(NSB - 1)
            act.wait_ge(unit_done, N_OUT)

            def mix_split(k):
                act.wait_ge(mixed_done, 4 * k + 4)
                nc.scalar.activation(xh[:, 4 * k:4 * k + 4, :].rearrange("p a b -> p (a b)"),
                                     mixed[:, k * D:(k + 1) * D], ACT.Copy).then_inc(mix_hi, 1)

            mix_split(0)
            weight_act(NSB - 1)
            for k in (1, 2, 3):
                mix_split(k)

            with act.Fori(0, N_PQ - N_OUT >> 1) as i:
                split_hi(act, N_OUT + 1, i, 2)
                split_hi(act, N_OUT + 2, i, 2)
            act.wait_ge(chunk_out, 8 + 16)
            norm_act(act, 1)

            def query_out(k, m, i=0):
                act.wait_ge(unit_done, k + 1 + 2 * i)
                nc.scalar.activation(qp[(m - M_PQ) % 2], gemm_bank[m % 2][:],
                                     ACT.Copy).then_inc(freed[m % 2], 1)

            def query_slot(j, i, first):
                if not first:
                    act.wait_ge(score_done, 2 * i + j - 1)
                query_out(N_PQ + j, M_PQ + j, i)

            split_hi(act, N_PQ + 1)
            act.wait_ge(xtok_done, 1)
            query_slot(0, 0, True)
            split_hi(act, N_PQ + 2)
            query_slot(1, 0, True)
            with act.Fori(1, PH) as i:
                for j in (0, 1):
                    split_hi(act, N_PQ + j + 1, i, 2)
                    query_slot(j, i, False)

            def gelu_act(k, m, slot, et, i=0, ks=0, ets=0):
                act.wait_ge(unit_done, k + 1 + ks * i)
                act.wait_ge(h_stored[slot], 16 + 8 * (et - slot) + 8 * ets * i)
                nc.scalar.activation(h_out[slot], gemm_bank[m % 2][:, 0:TD], ACT.Gelu).then_inc(freed[m % 2], 1)

            def weight_exp(n):
                act.wait_ge(diff_done, n)
                nc.scalar.activation(weight, weight, ACT.Exp).then_inc(gexp_done, 1)

            for k in range(TILES0):
                if k:
                    gelu_act(N_PRO + k - 1, M_PRO + k - 1, (k - 1) % 2, k - 1)
                split_hi(act, N_PRO + k + 1)
            weight_exp(1)
            with act.Fori(0, DB) as t:
                for j in range(TILES):
                    k = TILES0 + j
                    gelu_act(N_PRO + k - 1, M_PRO + k - 1, (k - 1) % 2, k - 1, t, TILES, TILES)
                    split_hi(act, N_PRO + k + 1, t, TILES)
                    if j == TILES - 5:
                        weight_exp(t + 2)
                    if j >= TILES - 4:
                        q = j - (TILES - 4)
                        act.wait_ge(gate_stored, t * 64 + 16 * (q + 1))
                        for b in range(8 * q, 8 * q + 8):
                            act.wait_ge(gate_done, t * 32 + b + 3)
                            nc.scalar.activation(
                                gate_piece.rearrange("p (i t) -> p t i", t=GT)[:, 4 * (b % 8):4 * (b % 8) + 4],
                                GATE_BANKS[b % 4][:].rearrange("p (t i) -> p t i", t=4),
                                ACT.Copy).then_inc(gate_out, 1)
            et = GRP * LAG - 1
            gelu_act(N_MAIN - 1, M_MAIN - 1, et % 2, et)

            def dots_gelu(ns, q, i=0, qs=0):
                act.wait_ge(gather_used, TICKETS + q + qs * i)
                nc.scalar.activation(dots[:, 0:ns], dots[:, 0:ns], ACT.Gelu).then_inc(dots_act, 1)

            def main_act(g):
                for k in range(8):
                    if 1 <= k <= 4:
                        gelu_act(N_MAIN + k - 1, M_MAIN + k - 1, (GRP * LAG + k - 1) % 2, GRP * LAG + k - 1,
                                 g, 8, 4)
                    split_hi(act, N_MAIN + k + 1, g, 8)
                    for j in range(2 * k, 2 * k + 2) if k < 2 else ():
                        act.wait_ge(w_gated, g * 4 + j + 1)
                        if j == 0:
                            act.wait_ge(unit_done, g * 8 + N_MAIN)
                        nc.scalar.activation(gh[:, j * TD:(j + 1) * TD], h_grp[:, j * TD:(j + 1) * TD],
                                             ACT.Copy).then_inc(w_hi, 1)
                    if k == 4:
                        dots_gelu(GM, GM, g, 2 * GM)

            with act.Fori(0, NMAIN) as g:
                main_act(g)

            def tail_w_act(i, r, first=False):
                if not first:
                    act.wait_ge(unit_done, i * 8 + (N_TAIL + 4 * (r - 1)))
                for j in range(GRP):
                    act.wait_ge(w_gated, i * 8 + (NMAIN + r) * 4 + j + 1)
                    nc.scalar.activation(xh[:, 4 * (r % 2) + j, 0:TD], h_grp[:, j * TD:(j + 1) * TD],
                                         ACT.Copy).then_inc(w_hi, 1)

            act.wait_ge(unit_done, N_TAIL - 4)
            tail_w_act(0, 0, True)

            with act.Fori(0, LAG // 2) as i:
                for r in range(2):
                    for c in range(CH):
                        split_hi(act, N_TAIL + 4 * r + c + 1, i, 8)
                        if c == 0:
                            tail_w_act(i, r + 1)
                        if c == 2:
                            dots_gelu(GTAIL[r], 2 * G_TAIL0 + (5 if r else 2), i, 6)
            for n in range(N_END - 3, N_END):
                split_hi(act, n)
                if n == N_END - 2:
                    dots_gelu(1, 2 * SLOTS - 1)

        @block.vector
        def _(dve):
            dve.wait_ge(const_ready, 1)
            dve.wait_ge(const_loaded, 16 * 5)
            dve.wait_ge(x_loaded, 16 * TB)
            nc.vector.tensor_scalar(qk_gain[:, 2:3], qk_gain[:, 0:1], SCALE, None, ALU.mult)
            norm_dve(dve, 0)

            def copy_out(k, dst, i=0, stride=0):
                dve.wait_ge(unit_done, k + 1 + stride * i)
                nc.vector.tensor_copy(dst, gemm_bank[k % 2][:]).then_inc(freed[k % 2], 1)

            def max_dve(p):
                for i in range(TB):
                    dve.wait_ge(logits_done, p * 4 + i + 1)
                    nc.vector.tensor_reduce(fox_stat[:, i:i + 1], banks[i][:, 0:(i + 1) * P], AX.X, ALU.max,
                                            negate=True).then_inc(nmax_done, 1)

            def prob_dve(p):
                for i in range(TB):
                    dve.wait_ge(exp_done, p * 4 + i + 1)
                    nc.vector.reciprocal(fox_stat[:, 8 + i:9 + i],
                                         fox_stat[:, 4 + i:5 + i]).then_inc(rsum_inv, 1)
                for i in range(TB):
                    dve.wait_ge(rsum_inv, p * 4 + i + 1)
                    nc.vector.tensor_scalar(fox_at(prob, i), fox_at(prob, i), fox_stat[:, 8 + i:9 + i],
                                            None, ALU.mult).then_inc(prob_done, 1)

            def vtok_dve(a):
                dve.wait_ge(vt_done, a + 1)
                nc.vector.tensor_copy(vtok, banks[7][:]).then_inc(vtok_done, 1)

            def turned_dve(p):
                for j in range(TB):
                    dve.wait_ge(pt_done, p * 4 + j + 1)
                    nc.vector.tensor_copy(col_at(probT, j), banks[j][:, 0:(TB - j) * P]).then_inc(pt_out, 1)

            def gate_dve(p):
                dve.wait_ge(freed[0], p * 2 + 3)
                nc.vector.tensor_scalar(gT, gT, 1.0, None, ALU.add).then_inc(gate_step, 1)
                dve.wait_ge(gate_step, p * 2 + 1)
                nc.vector.reciprocal(gT, gT).then_inc(gate_step, 1)
                dve.wait_ge(gate_step, p * 2 + 2)
                dve.wait_ge(o_done, p + 1)
                nc.vector.tensor_tensor(mixed_at(p), banks[6][:], gT, ALU.mult).then_inc(mixed_done, 1)

            def decay_dve(h):
                wait_from(dve, logits_done, h * 4)
                pick = sel[:, h:h + 1] if isinstance(h, int) else sel[:, bass.ds(h, 1)]
                nc.vector.tensor_scalar(cl[0:PH], csum, pick, None, ALU.mult)
                nc.vector.tensor_scalar(cr[32:32 + PH], csum, pick, None, ALU.mult).then_inc(c_ready, 1)

            def rms_dve(h):
                for c, buf in enumerate((q_sq, k_sq)):
                    dve.wait_ge(rms_done, h * 2 + c + 1)
                    nc.vector.reciprocal(buf, buf).then_inc(rinv_done, 1)
                for c, (buf, src, dst) in enumerate(((q_sq, q_raw, qn), (k_sq, k_raw, kn))):
                    dve.wait_ge(rinv_done, h * 2 + c + 1)
                    nc.vector.scalar_tensor_tensor(out=dst, in0=src, scalar=qk_gain[:, 2 - c:3 - c], in1=buf,
                                                   op0=ALU.mult, op1=ALU.mult).then_inc(qk_normed, 1)

            def fox_dve(h, p):
                if p is not None:
                    max_dve(p)
                    prob_dve(p)
                else:
                    dve.wait_ge(unit_done, 1)
                    nc.vector.tensor_scalar(flog, gemm_bank[0][0:PH, :], bf[:, 0:1], None,
                                            ALU.add).then_inc(freed[0], 1)
                copy_out(1, q_raw, h, 4)
                if p is not None:
                    vtok_dve(p)
                copy_out(2, k_raw, h, 4)
                if p is not None:
                    turned_dve(p)
                    gate_dve(p)
                else:
                    dve.wait_ge(act_step, 3)
                    nc.vector.scalar_tensor_tensor(out=flog, in0=flog, scalar=0.0, in1=ftmp, op0=ALU.min,
                                                   op1=ALU.subtract).then_inc(dve_step, 1)
                    dve.wait_ge(dve_step, 1)
                    nc.vector.tensor_tensor_scan(csum, cr[0:PH], flog, 0.0, ALU.mult,
                                                 ALU.add).then_inc(csum_done, 1)
                    dve.wait_ge(csum_done, 1)
                decay_dve(h)
                rms_dve(h)

            fox_dve(0, None)
            fox_dve(1, 0)
            with dve.Fori(2, NFOX) as h:
                fox_dve(h, h - 1)

            def softplus_dve(s):
                dve.wait_ge(ln_step, s * 2 + 2)
                for j in range(TB):
                    nc.vector.scalar_tensor_tensor(out=col_at(sp_, j), in0=banks[j][:, 0:(TB - j) * P],
                                                   scalar=0.0, in1=col_at(prob, j), op0=ALU.max,
                                                   op1=ALU.add).then_inc(sp_done, 1)
                for j in range(TB):
                    dve.wait_ge(sp_done, s * 8 + j + 1)
                    diag = col_at(sp_, j)[:, 0:P]
                    nc.vector.tensor_tensor(diag, diag, strict, ALU.mult).then_inc(sp_done, 1)

            def mixed_dve(s):
                dve.wait_ge(o_done, s + (NFOX + 1))
                nc.vector.tensor_copy(mixed_at(s + NFOX), banks[6][:]).then_inc(mixed_done, 1)

            def stick_pair_dve(i, peeled):
                for r in range(2):
                    k = N_SB + 3 * r
                    s = i * 2 + r
                    if peeled and r == 0:
                        max_dve(NFOX - 1)
                        prob_dve(NFOX - 1)
                        vtok_dve(NFOX - 1)
                        turned_dve(NFOX - 1)
                        copy_out(k + 1, kn)
                        gate_dve(NFOX - 1)
                    else:
                        softplus_dve(s - 1)
                        vtok_dve(s + (NFOX - 1))
                        copy_out(k + 1, kn, i, 6)
                        mixed_dve(s - 1)

            stick_pair_dve(0, True)
            with dve.Fori(1, NSB // 2) as i:
                stick_pair_dve(i, False)
            softplus_dve(NSB - 1)
            vtok_dve(HEADS - 1)

            def mix_rest(k):
                dve.wait_ge(mix_hi, k + 1)
                nc.vector.tensor_tensor(xl[:, 4 * k:4 * k + 4, :].rearrange("p a b -> p (a b)"),
                                        mixed[:, k * D:(k + 1) * D],
                                        xh[:, 4 * k:4 * k + 4, :].rearrange("p a b -> p (a b)").bitcast(F32),
                                        ALU.subtract).then_inc(mix_lo, 1)

            mix_rest(0)
            mixed_dve(NSB - 1)
            nc.vector.memset(stat[:, 12:13], 0.0).then_inc(chunk_out, 8)
            for k in (1, 2, 3):
                mix_rest(k)

            dve.wait_ge(x_loaded, 2 * 16 * TB)
            with dve.Fori(0, 2) as w:
                for r in range(2):
                    add_chunk(dve, N_OUT + 4 * r + 3, 3 * r, w * 2 + r, CHUNK_BANKS[r], w, 8, 6)
            dve.wait_ge(chunk_out, 8 + 16)
            norm_dve(dve, 1)
            dve.wait_ge(const_loaded, 16 * 6)
            dve.wait_ge(row_scaled, 2 * TB)
            nc.vector.tensor_tensor(x_tok, rows[1], gain_row, ALU.mult).then_inc(xtok_done, 1)
            nc.vector.memset(stat[:, 13:14], 0.0).then_inc(gate_out, len(GATE_BANKS))
            nc.vector.memset(stat[:, 14:15], 0.0).then_inc(gate_done, 2)

            def score_out_dve(j, i=0):
                dve.wait_ge(score_done, i * 2 + j + 1)
                if not isinstance(i, int):
                    dve.wait_ge(score_stored[j], i * 16)
                nc.vector.tensor_copy(s_out[j], banks[j][:]).then_inc(score_out, 1)

            score_out_dve(0)
            score_out_dve(1)
            with dve.Fori(1, PH) as i:
                score_out_dve(0, i)
                score_out_dve(1, i)

            def choice_dve(nth, t=None):
                count = [0]

                def step(ins):
                    count[0] += 1
                    ins.then_inc(topk_step, 1)
                    wait_apart(dve, topk_step, nth * TOPK_STEPS + count[0])

                halves = [(h, c) for h in range(PH) for c in range(2)]

                def s_of(h, c):
                    return s_cur[:, (2 * h + c) * NKEYS:(2 * h + c + 1) * NKEYS]

                wait_apart(dve, cur_loaded, nth * 16 + 16)
                for r in range(2):
                    e = slice(8 * r, 8 * r + 8)
                    for h, c in halves:
                        last = nc.vector.max(top_v[:, h, c, e], s_of(h, c))
                    step(last)
                    for h, c in halves:
                        last = nc.vector.max_index(top_i[:, h, c, e], top_v[:, h, c, e], s_of(h, c))
                    step(last)
                    if r == 0:
                        for h, c in halves:
                            last = nc.vector.match_replace(s_of(h, c), top_v[:, h, c, e], s_of(h, c), LOWEST)
                        step(last)
                cand = s_cur.rearrange("p (h a b) -> p h a b", h=PH, a=TOPK)
                cand_of = [s_cur[:, 256 * h:256 * h + 256] for h in range(PH)]
                best_h = best.rearrange("p (h k) -> p h k", h=PH)
                weight_h = weight.rearrange("p (h k) -> p h k", h=PH)
                pos_h = pos.rearrange("p (h k) -> p h k", h=PH)
                step(nc.vector.tensor_tensor(cand, top_v[:, :, 0, :].unsqueeze(3).broadcast_to([P, PH, TOPK, TOPK]),
                                             top_v[:, :, 1, :].unsqueeze(2).broadcast_to([P, PH, TOPK, TOPK]),
                                             ALU.add))
                for r in range(2):
                    e = slice(8 * r, 8 * r + 8)
                    for h in range(PH):
                        last = nc.vector.max(best_h[:, h, e], cand_of[h])
                    step(last)
                    for h in range(PH):
                        last = nc.vector.max_index(pos_h[:, h, e], best_h[:, h, e], cand_of[h])
                    step(last)
                    if r == 0:
                        for h in range(PH):
                            last = nc.vector.match_replace(cand_of[h], best_h[:, h, e], cand_of[h], LOWEST)
                        step(last)
                nc.vector.tensor_tensor(weight_h, best_h, best_h[:, :, 0:1].broadcast_to([P, PH, TOPK]),
                                        ALU.subtract).then_inc(diff_done, 1)
                nc.vector.tensor_scalar(pos2[:, 0:128], pos, 4, None, ALU.logical_shift_right)
                nc.vector.tensor_scalar(pos2[:, 128:256], pos, 15, None, ALU.bitwise_and)
                step(nc.vector.tensor_copy(top_if, top_i.rearrange("p h c k -> p (h c k)")))
                step(nc.vector.tensor_copy(pos2f, pos2))
                look = s_cur.rearrange("p (h k j) -> p h k j", h=PH, k=TOPK)
                look_s = s_cur.rearrange("p (s j) -> p s j", j=TOPK)
                idx_f = top_if.rearrange("p (h c k) -> p h c k", h=PH, c=2)
                for c in range(2):
                    step(nc.vector.tensor_tensor(
                        look_s, pos2f[:, 128 * c:128 * c + 128].unsqueeze(2).broadcast_to([P, P, TOPK]),
                        iota16[:].unsqueeze(1).broadcast_to([P, P, TOPK]), ALU.is_equal))
                    step(nc.vector.tensor_tensor(
                        look, look, idx_f[:, :, c, :].unsqueeze(2).broadcast_to([P, PH, TOPK, TOPK]), ALU.mult))
                    step(nc.vector.tensor_reduce(slots[:, c, :], look_s, AX.X, ALU.add))
                dve.wait_ge(gexp_done, nth + 1)
                step(nc.vector.tensor_reduce(gsum[:, 0:PH], weight_h, AX.X, ALU.add))
                step(nc.vector.reciprocal(gsum[:, PH:2 * PH], gsum[:, 0:PH]))
                assert count[0] == TOPK_STEPS, count[0]
                gate_of = g_wt[:] if t is None else slots[:, 2, :]
                gate_ins = nc.vector.tensor_tensor(gate_of.rearrange("p (h k) -> p h k", h=PH), weight_h,
                                                   gsum[:, PH:2 * PH].unsqueeze(2).broadcast_to([P, PH, TOPK]),
                                                   ALU.mult)
                if t is None:
                    gate_ins.then_inc(gwt_done, 1)
                    nc.vector.scalar_tensor_tensor(out=g_idx[:], in0=slots[:, 0, :], scalar=float(NKEYS),
                                                   in1=slots[:, 1, :], op0=ALU.mult,
                                                   op1=ALU.add).then_inc(chosen_done, 1)
                    return
                gate_ins.then_inc(slots_done, 1)
                dve.wait_ge(slots_turned, t + 1)
                nc.vector.tensor_copy(slotT.rearrange("p a b -> p (a b)"), banks[0][:, 0:3 * P]
                                      ).then_inc(slotT_done, 1)
                dve.wait_ge(slotT_done, t + 1)
                for b in range(32):
                    dve.wait_ge(gate_done, t * 32 + b + 1)
                    nc.vector.tensor_tensor(
                        gh[:, (b % 2) * 512:(b % 2) * 512 + 512].rearrange("p (t n) -> p t n", t=4),
                        iota128[:].unsqueeze(1).broadcast_to([P, 4, NKEYS]),
                        slotT[:, 1, 4 * b:4 * b + 4].unsqueeze(2).broadcast_to([P, 4, NKEYS]), ALU.is_equal)
                    for j in range(4):
                        n = 4 * b + j
                        last = nc.vector.tensor_scalar(hot_gate[b % 2][:, j * P:(j + 1) * P], iota128[:],
                                                       slotT[:, 0, n:n + 1], slotT[:, 2, n:n + 1],
                                                       ALU.is_equal, ALU.mult)
                    last.then_inc(hot_done, 1)
                nc.vector.memset(stat[:, 15:16], 0.0).then_inc(chosen_done, 1)

            choice_dve(0)
            with dve.Fori(0, DB) as t:
                choice_dve(t + 1, t)

            def gate_mult(g):
                dve.wait_ge(grp_loaded, g * 32 + 32)
                for j in range(GRP):
                    mine = h_grp[:, j * TD:(j + 1) * TD].rearrange("p (c t) -> p c t", c=NGC)
                    nc.vector.tensor_tensor(
                        mine, mine, g_grp.rearrange("p (c e t) -> p c e t", c=NGC, e=GRP)[:, :, j, :],
                        ALU.mult).then_inc(w_gated, 1)

            def gate_rest(g, hi_of, lo_of):
                for j in range(GRP):
                    dve.wait_ge(w_hi, g * 4 + j + 1)
                    nc.vector.tensor_tensor(lo_of(j), h_grp[:, j * TD:(j + 1) * TD], hi_of(j).bitcast(F32),
                                            ALU.subtract).then_inc(w_lo, 1)

            def slots_of(buf, s0, ns, i, ss):
                s = i * ss + s0
                return buf[:, s:s + ns] if isinstance(s, int) else buf[:, bass.ds(s, ns)]

            def set_idx(idx, ready, s0, ns, i=0, ss=0):
                nc.vector.tensor_copy(idx[:, 0:ns], slots_of(g_idx, s0, ns, i, ss)).then_inc(ready, 1)

            def dot(j, place):
                q, b, filled, _ = place
                dve.wait_ge(gathered[b], filled * 16)
                nc.vector.tensor_tensor_reduce(out=rows_g[b], in0=rows_g[b], in1=x_tok, scale=1.0,
                                               scalar=0.0, op0=ALU.mult, op1=ALU.add,
                                               accum_out=dots[:, j:j + 1]).then_inc(gather_used, 1)

            def coefs(s0, ns, n, i=0, ss=0, gs=0):
                dve.wait_ge(dots_act, n + 1 + gs * i)
                nc.vector.tensor_tensor(dots[:, GM:GM + ns], dots[:, 0:ns], slots_of(g_wt, s0, ns, i, ss),
                                        ALU.mult).then_inc(coef_done, 1)
                dve.wait_ge(coef_done, n + 1 + gs * i)

            def add_row(j, place):
                q, b, filled, _ = place
                dve.wait_ge(gathered[b], filled * 16)
                dve.wait_ge(gather_used, q + TICKETS)
                nc.vector.scalar_tensor_tensor(out=acc[:, DB, :], in0=rows_g[b],
                                               scalar=dots[:, GM + j:GM + j + 1], in1=acc[:, DB, :],
                                               op0=ALU.mult, op1=ALU.add).then_inc(gather_used, 1)

            dve.wait_ge(chosen_done, 1)
            dve.wait_ge(gwt_done, 1)
            set_idx(idx_u, idx_u_ready, 0, GM)

            def tail_mult(i, r):
                gate_mult(i * 2 + (NMAIN + r))

            def tail_rest(i, r):
                b = 4 * (r % 2)
                gate_rest(i * 2 + (NMAIN + r), lambda j: xh[:, b + j, 0:TD], lambda j: xl[:, b + j, 0:TD])

            def main_dve(g, last):
                def d(j):
                    dot(j, in_main(j, g))

                def r(j):
                    add_row(j, in_main(GM + j, g))

                def chunk(c):
                    add_chunk(dve, N_MAIN + GRP + c, 12 + 2 * c, c, DENSE_BANKS[c % 2], g, 8, 8)

                set_idx(idx_v, idx_v_ready, 0, GM, g, GM)
                gate_mult(g)
                d(0)
                gate_rest(g, lambda j: gh[:, j * TD:(j + 1) * TD], lambda j: gl[:, j * TD:(j + 1) * TD])
                for j in range(1, GM):
                    d(j)
                if last:
                    set_idx(idx_u, idx_u_ready, G_TAIL0, GTAIL[0])
                else:
                    set_idx(idx_u, idx_u_ready, GM, GM, g, GM)
                coefs(0, GM, 0, g, GM, 1)
                r(0)
                for c in range(CH):
                    if last and c == 2:
                        tail_mult(0, 0)
                    chunk(c)
                    if last and c == 2:
                        tail_rest(0, 0)
                    r(c + 1)

            with dve.Fori(0, NMAIN - 1) as g:
                main_dve(g, False)
            main_dve(NMAIN - 1, True)

            def tail_dve(i, r, next_ns):
                ns, s0 = GTAIL[r], G_TAIL0 + r * GTAIL[0]
                j0 = 4 * r
                set_idx(idx_v, idx_v_ready, s0, ns, i, 3)
                tail_mult(i, r + 1)
                dot(0, in_tail(j0, i))
                tail_rest(i, r + 1)
                if ns > 1:
                    dot(1, in_tail(j0 + 1, i))
                set_idx(idx_u, idx_u_ready, s0 + ns, next_ns, i, 3)
                for c in range(CH):
                    if c == 2:
                        coefs(s0, ns, NMAIN + r, i, 3, 2)
                    if 2 <= c < ns + 2:
                        add_row(c - 2, in_tail(j0 + ns + c - 2, i))
                    add_chunk(dve, N_TAIL + 4 * r + c, 12 + 8 * (NMAIN + r) + 2 * c, c, DENSE_BANKS[c % 2], i,
                              8, 16)

            with dve.Fori(0, LAG // 2 - 1) as i:
                tail_dve(i, 0, GTAIL[1])
                tail_dve(i, 1, GTAIL[0])
            tail_dve(LAG // 2 - 1, 0, GTAIL[1])
            tail_dve(LAG // 2 - 1, 1, 1)
            s0 = SLOTS - 1
            set_idx(idx_v, idx_v_ready, s0, 1)
            dot(0, in_tail(0, LAG // 2))
            for c in range(CH):
                if c == 2:
                    coefs(s0, 1, NGRP - 1)
                    add_row(0, in_tail(1, LAG // 2))
                add_chunk(dve, N_END - CH + c, 12 + 8 * (NGRP - 1) + 2 * c, c, DENSE_BANKS[c % 2])

        @block.tensor
        def _(pe):
            pe.wait_ge(const_ready, 1)
            norm_pe(pe, 0)
            pe.wait_ge(xl_done, 16)
            gemm(pe, 0, 0)

            def sumsq_pe(h):
                for c, buf in enumerate((q_sq, k_sq)):
                    pe.wait_ge(sq_done, h * 2 + c + 1)
                    if c == 0:
                        wait_from(pe, pt_out, h * 4)
                    nc.tensor.matmul(banks[c][:], ones[:], buf, start=True, stop=True).then_inc(ss_done, 1)

            def logits_pe(p):
                pe.wait_ge(qk_normed, p * 2 + 2)
                pe.wait_ge(c_ready, p + 1)
                for i in range(TB):
                    n = (i + 1) * P
                    qs = slice(i * P, n)
                    nc.tensor.matmul(banks[i][:, 0:n], qn[:, qs], kn[:, 0:n], start=True, stop=False)
                    nc.tensor.matmul(banks[i][:, 0:n], cl[0:32 + PH, qs], cr[0:32 + PH, 0:n],
                                     start=False, stop=False)
                    nc.tensor.matmul(banks[i][:, qs], ident_b, fox_mask, start=False,
                                     stop=True).then_inc(logits_done, 1)

            def vturn_pe(a, k, i=0, stride=0):
                evacuated(pe, k, i, stride)
                wait_from(pe, vtok_done, a)
                for j in range(TB):
                    mm = nc.tensor.transpose(banks[7][:, j * P:(j + 1) * P], vT[:, j * P:(j + 1) * P], ident[:])
                mm.then_inc(vt_done, 1)

            def pturn_pe(p):
                pe.wait_ge(prob_done, p * 4 + 4)
                for j in range(TB):
                    for i in range(j, TB):
                        mm = nc.tensor.transpose(banks[j][:, (i - j) * P:(i - j + 1) * P],
                                                 fox_at(prob, i)[:, j * P:(j + 1) * P], ident[:])
                    mm.then_inc(pt_done, 1)

            def out_pe(a, ready, n):
                pe.wait_ge(ready, n)
                pe.wait_ge(vtok_done, a + 1)
                wait_from(pe, mixed_done, a)
                for j in range(TB):
                    mm = nc.tensor.matmul(banks[6][:, j * P:T], vtok[:, j * P:(j + 1) * P], col_at(probT, j),
                                          start=(j == 0), stop=(j == TB - 1))
                mm.then_inc(o_done, 1)

            def fox_pe(h, p):
                if p is not None:
                    logits_pe(p)
                gemm(pe, 1, 1, h, 4, 4)
                if p is not None:
                    vturn_pe(p, 3, p, 4)
                gemm(pe, 2, 2, h, 4, 4)
                if p is not None:
                    pturn_pe(p)
                gemm(pe, 3, 3, h, 4, 4)
                if p is not None:
                    out_pe(p, pt_out, p * 4 + 4)
                sumsq_pe(h)
                gemm(pe, 4, 4, h, 4, 4)

            fox_pe(0, None)
            fox_pe(1, 0)
            with pe.Fori(2, NFOX) as h:
                fox_pe(h, h - 1)

            def z_pe(s, k, i=0):
                evacuated(pe, k, i, 6)
                evacuated(pe, k + 1, i, 6)
                if isinstance(s, int) and s == 0:
                    pe.wait_ge(pt_out, 4 * NFOX)
                else:
                    pe.wait_ge(at_done, s * 4)
                for j in range(TB):
                    nc.tensor.matmul(banks[j][:, 0:(TB - j) * P], kn[:, j * P:(j + 1) * P], qn[:, j * P:T],
                                     start=True, stop=True).then_inc(zt_done, 1)

            def tri_pe(s):
                pe.wait_ge(sp_done, s * 8 + 8)
                for j in range(TB):
                    nc.tensor.matmul(banks[j][:, 0:(TB - j) * P], neg_tri, col_at(sp_, j), start=False,
                                     stop=False, skip_group_check=True)
                    for l in range(j + 1, TB):
                        nc.tensor.matmul(banks[j][:, (l - j) * P:(TB - j) * P], neg_ones, col_at(sp_, l),
                                         start=False, stop=False, skip_group_check=True)
                    nc.tensor.matmul(banks[j][:, 0:P], ident_b, sb_mask, start=False, stop=True,
                                     skip_group_check=True).then_inc(tri_done, 1)

            def stick_pair_pe(i, peeled):
                for r in range(2):
                    k = N_SB + 3 * r
                    s = i * 2 + r
                    if peeled and r == 0:
                        logits_pe(NFOX - 1)
                        gemm(pe, k, k)
                        vturn_pe(NFOX - 1, 3, NFOX - 1, 4)
                        pturn_pe(NFOX - 1)
                        gemm(pe, k + 1, k + 1)
                        out_pe(NFOX - 1, pt_out, 4 * NFOX)
                        gemm(pe, k + 2, k + 2)
                    else:
                        z_pe(s - 1, k - 3, i)
                        gemm(pe, k, k, i, 6, 6)
                        vturn_pe(s + (NFOX - 1), k - 1, i, 6)
                        tri_pe(s - 1)
                        gemm(pe, k + 1, k + 1, i, 6, 6)
                        out_pe(s + (NFOX - 1), at_done, s * 4)
                        gemm(pe, k + 2, k + 2, i, 6, 6)

            stick_pair_pe(0, True)
            with pe.Fori(1, NSB // 2) as i:
                stick_pair_pe(i, False)
            z_pe(NSB - 1, N_OUT - 3)
            vturn_pe(HEADS - 1, N_OUT - 1)
            tri_pe(NSB - 1)
            out_pe(HEADS - 1, at_done, 4 * NSB)

            with pe.Fori(0, 2) as w:
                for r in range(2):
                    for q in range(4):
                        pe.wait_ge(mix_lo, q + 1)
                        chunk_unit(pe, N_OUT + 4 * r + q, CHUNK_BANKS[r], q == 0, q == 3,
                                   lambda e: xh[:, 4 * q + e, :], lambda e: xl[:, 4 * q + e, :],
                                   lambda tb: pe.wait_ge(chunk_out, w * 8 + 4 * r + tb + 1), w, 8)
            norm_pe(pe, 1)
            pe.wait_ge(xl_done, 32)

            def score_pe(j, i=0):
                evacuated(pe, M_PQ + j, i, 2)
                wait_from(pe, score_out, i * 2 + (j - 1))
                b = j % 2
                for tb in range(TB):
                    n = i * 2 + j
                    mm = nc.tensor.matmul(banks[b][:, tb * P:(tb + 1) * P], qp[b][:, tb * P:(tb + 1) * P],
                                          keysT[:, n, :], start=True, stop=True)
                mm.then_inc(score_done, 1)

            gemm(pe, N_PQ, M_PQ)
            gemm(pe, N_PQ + 1, M_PQ + 1)
            pe.wait_ge(keys_loaded, 16)
            for j in range(2):
                score_pe(j)
                gemm(pe, N_PQ + 2 + j, M_PQ + 2 + j)
            with pe.Fori(1, PH - 1) as i:
                for j in range(2):
                    score_pe(j, i)
                    gemm(pe, N_PQ + 2 + j, M_PQ + 2 + j, i, 2, 2)
            score_pe(0, PH - 1)
            score_pe(1, PH - 1)

            for k in range(TILES0):
                gemm(pe, N_PRO + k, M_PRO + k, width=TD)

            def gate_batch(t, b):
                pe.wait_ge(hot_done, t * 32 + b + 1)
                pe.wait_ge(gate_out, t * 32 + b + 1)
                for n in range(4):
                    mm = nc.tensor.matmul(GATE_BANKS[b % 4][:, n * P:(n + 1) * P],
                                          gh[:, (b % 2) * 512 + n * P:(b % 2) * 512 + (n + 1) * P].bitcast(F32),
                                          hot_gate[b % 2][:, n * P:(n + 1) * P], start=True, stop=True)
                mm.then_inc(gate_done, 1)

            with pe.Fori(0, DB) as t:
                for j in range(TILES):
                    q = j - (TILES - 4)
                    if q == 0:
                        pe.wait_ge(slots_done, t + 1)
                        for a in range(3):
                            mm = nc.tensor.transpose(banks[0][:, a * P:(a + 1) * P], slots[:, a, :], ident[:])
                        mm.then_inc(slots_turned, 1)

                    def between(part):
                        for b in ((), (), (0,), (1,), (2,), (3,), (4, 5), (6, 7))[part]:
                            gate_batch(t, 8 * q + b)

                    gemm(pe, N_PRO + TILES0 + j, M_PRO + TILES0 + j, t, TILES, TILES, TD,
                         between if q >= 0 else None)
            pe.wait_ge(gate_out, DB * 32 + len(GATE_BANKS))

            def v_chunk(k, d, c, a_hi, a_lo, i, stride, dstride):
                chunk_unit(pe, k, DENSE_BANKS[c % 2], True, True, a_hi, a_lo,
                           lambda tb: pe.wait_ge(chunk_out, 19 + 3 * d + tb + 3 * dstride * i), i, stride)

            with pe.Fori(0, NMAIN) as g:
                for k in range(GRP):
                    gemm(pe, N_MAIN + k, M_MAIN + k, g, 8, 4, TD)
                pe.wait_ge(w_lo, g * 4 + 4)
                for c in range(CH):
                    v_chunk(N_MAIN + GRP + c, c, c, lambda e: gh[:, e * TD:(e + 1) * TD],
                            lambda e: gl[:, e * TD:(e + 1) * TD], g, 8, 4)

            def tail_pe(i, r):
                pe.wait_ge(w_lo, i * 8 + 4 * (NMAIN + r + 1))
                w = 4 * (r % 2)
                for c in range(CH):
                    v_chunk(N_TAIL + 4 * r + c, 4 * (NMAIN + r) + c, c, lambda e: xh[:, w + e, 0:TD],
                            lambda e: xl[:, w + e, 0:TD], i, 8, 8)

            with pe.Fori(0, LAG // 2) as i:
                tail_pe(i, 0)
                tail_pe(i, 1)
            tail_pe(LAG // 2, 0)


_INS = ["x", "attn_g", "w_in", "b_forget", "q_g", "k_g", "w_out", "ffn_g", "ffn_row", "w_pq",
        "sub_keys", "u", "v", "u_rows", "v_rows"]


def kernel(x, attn_norm_g, w_in, b_forget, q_norm_g, k_norm_g, w_out, ffn_norm_g, w_peer_q,
           peer_sub_keys, peer_u, peer_v):
    import numpy as np
    import concourse.bacc as bacc
    from concourse.bass_utils import run_bass_kernel_spmd

    def arr(a):
        return np.asarray(a)

    def units(w):
        return np.ascontiguousarray(w.reshape(KC, P, -1, P).transpose(2, 1, 0, 3)).reshape(-1, P, D)

    wi = arr(w_in)[0]
    d1 = NFOX * HD
    cols = [np.arange(7 * d1, 7 * d1 + PH), np.arange(P - PH)]
    for h in range(NFOX):
        cols += [np.arange(s * d1 + h * HD, s * d1 + (h + 1) * HD) for s in range(4)]
    for h in range(NSB):
        cols += [np.arange((4 + s) * d1 + h * HD, (4 + s) * d1 + (h + 1) * HD) for s in range(3)]
    data = {
        "x": arr(x)[0],
        "attn_g": np.ascontiguousarray(arr(attn_norm_g)[0].reshape(KC, P).T),
        "w_in": units(wi[:, np.concatenate(cols)]),
        "b_forget": arr(b_forget)[0].reshape(PH, 1),
        "q_g": arr(q_norm_g)[0].reshape(P, 1),
        "k_g": arr(k_norm_g)[0].reshape(P, 1),
        "w_out": np.ascontiguousarray(arr(w_out)[0].reshape(4, 4, P, CH, 512).transpose(3, 0, 2, 1, 4)
                                      ).reshape(-1, P, D),
        "ffn_g": np.ascontiguousarray(arr(ffn_norm_g)[0].reshape(KC, P).T),
        "ffn_row": arr(ffn_norm_g)[0],
        "w_pq": units(arr(w_peer_q)[0]),
        "sub_keys": np.ascontiguousarray(arr(peer_sub_keys)[0].reshape(2 * PH, NKEYS, P).transpose(2, 0, 1)),
        "u": np.ascontiguousarray(arr(peer_u)[0].reshape(NKEYS, P, KC, P).transpose(0, 3, 2, 1)
                                  ).reshape(NKEYS, P, D),
        "v": np.ascontiguousarray(arr(peer_v)[0].reshape(NGRP, GRP, P, CH, 512).transpose(0, 3, 2, 1, 4)
                                  ).reshape(-1, P, D),
        "u_rows": arr(peer_u)[0],
        "v_rows": arr(peer_v)[0],
    }
    nc = bacc.Bacc("TRN2", target_bir_lowering=False, num_devices=1)
    args, arrays = [], {}
    for name in _INS:
        a = np.ascontiguousarray(data[name])
        arrays[f"in_{name}"] = a
        args.append(nc.dram_tensor(f"in_{name}", a.shape, mybir.dt.from_np(a.dtype), kind="ExternalInput").ap())
    args.append(nc.dram_tensor("out_y", (T, D), F32, kind="ExternalOutput").ap())
    build(nc, *args)
    nc.compile()
    r = run_bass_kernel_spmd(nc, [arrays], core_ids=[0])
    return r.results[0]["out_y"].reshape(1, T, D)
```
